# Optimizing a Trainium2 kernel written in Bass

```python
import jax, jax.numpy as jnp
from jax import lax
import numpy as np

D_MODEL = 1024
BATCH = 1
SEQ = 512
DEPTH = 1

D_CONV = D_MODEL
CONV_WIDTH = 3
HEAD_DIM = 64
N_HEADS = D_MODEL // HEAD_DIM
N_KV_HEADS = N_HEADS // 8
GROUP = N_HEADS // N_KV_HEADS
WINDOW = 128
BLOCK = 128
N_BUCKETS = 32
MAX_DISTANCE = 128
D_FF = 4 * D_MODEL
EPS = 1e-6
NEG_INF = -1e30

Q_COLS = N_HEADS * HEAD_DIM
KV_COLS = N_KV_HEADS * HEAD_DIM
IN_COLS = 3 * D_CONV + Q_COLS + 2 * KV_COLS + 2 * D_MODEL
SPLITS = (D_CONV, 2 * D_CONV, 3 * D_CONV,
          3 * D_CONV + Q_COLS,
          3 * D_CONV + Q_COLS + KV_COLS,
          3 * D_CONV + Q_COLS + 2 * KV_COLS,
          3 * D_CONV + Q_COLS + 2 * KV_COLS + D_MODEL)

kernel_name = "hybrid_conv_swa_gated_block"

def rmsnorm(x, g):
    xf = x.astype(jnp.float32)
    y = xf * lax.rsqrt(jnp.mean(xf * xf, axis=-1, keepdims=True) + EPS)
    return (y * g.astype(jnp.float32)).astype(x.dtype)

def t5_causal_bucket(dist):
    n = np.maximum(dist, 0)
    max_exact = N_BUCKETS // 2
    ratio = np.log(np.maximum(n, max_exact).astype(np.float32) / max_exact) / np.log(MAX_DISTANCE / max_exact)
    large = max_exact + (ratio * (N_BUCKETS - max_exact)).astype(np.int32)
    large = np.minimum(large, N_BUCKETS - 1)
    return np.where(n < max_exact, n, large).astype(np.int32)

def short_conv(u, w):
    c = u.shape[-1]
    return lax.conv_general_dilated(
        u, w[:, None, :].astype(u.dtype), window_strides=(1,),
        padding=[(CONV_WIDTH - 1, 0)],
        dimension_numbers=("NWC", "WIO", "NWC"),
        feature_group_count=c)

def sliding_window_attention(q, k, v, sinks, rel_bias):
    b, t = q.shape[0], q.shape[1]
    nb = t // BLOCK
    qb = q.reshape(b, nb, BLOCK, N_KV_HEADS, GROUP, HEAD_DIM)
    pad = ((0, 0), (BLOCK, 0), (0, 0), (0, 0))
    kp = jnp.pad(k, pad).reshape(b, nb + 1, BLOCK, N_KV_HEADS, HEAD_DIM)
    vp = jnp.pad(v, pad).reshape(b, nb + 1, BLOCK, N_KV_HEADS, HEAD_DIM)
    kb = jnp.concatenate([kp[:, :-1], kp[:, 1:]], axis=2)
    vb = jnp.concatenate([vp[:, :-1], vp[:, 1:]], axis=2)

    s = jnp.einsum("bnqkgd,bnskd->bnkgqs", qb, kb).astype(jnp.float32) * (HEAD_DIM ** -0.5)

    qi = np.arange(BLOCK)[:, None]
    kj = np.arange(2 * BLOCK)[None, :]
    dist = qi + BLOCK - kj
    in_window = (dist >= 0) & (dist < WINDOW)
    bias = rel_bias.astype(jnp.float32)[t5_causal_bucket(dist)]
    bias = jnp.transpose(bias, (2, 0, 1)).reshape(N_KV_HEADS, GROUP, BLOCK, 2 * BLOCK)
    key_pos = np.arange(nb)[:, None] * BLOCK + kj - BLOCK
    mask = in_window[None] & (key_pos >= 0)[:, None, :]
    s = jnp.where(mask[:, None, None], s + bias, NEG_INF)

    sink = jnp.broadcast_to(sinks.astype(jnp.float32).reshape(N_KV_HEADS, GROUP, 1, 1),
                            s.shape[:-1] + (1,))
    p = jax.nn.softmax(jnp.concatenate([s, sink], axis=-1), axis=-1)[..., :-1]
    o = jnp.einsum("bnkgqs,bnskd->bnqkgd", p.astype(vb.dtype), vb)
    return o.reshape(b, t, N_HEADS * HEAD_DIM)

def setup_inputs(seed: int = 0) -> dict:
    key = jax.random.key(seed)
    ks = jax.random.split(key, 14)
    f32 = jnp.float32
    nrm = lambda k, shape, scale: jax.random.normal(k, shape, f32) * scale
    return {
        "x": nrm(ks[0], (BATCH, SEQ, D_MODEL), 1.0),
        "attn_norm_g": 1.0 + nrm(ks[1], (DEPTH, D_MODEL), 0.05),
        "w_in": nrm(ks[2], (DEPTH, D_MODEL, IN_COLS), D_MODEL ** -0.5),
        "conv_w": nrm(ks[3], (DEPTH, CONV_WIDTH, D_CONV), CONV_WIDTH ** -0.5),
        "w_conv_out": nrm(ks[4], (DEPTH, D_CONV, D_MODEL), D_CONV ** -0.5),
        "attn_sinks": nrm(ks[5], (DEPTH, N_HEADS), 0.5),
        "rel_bias": nrm(ks[6], (N_BUCKETS, N_HEADS), 0.5),
        "w_attn_out": nrm(ks[7], (DEPTH, Q_COLS, D_MODEL), Q_COLS ** -0.5),
        "w_o": nrm(ks[8], (DEPTH, D_MODEL, D_MODEL), D_MODEL ** -0.5),
        "mlp_norm_g": 1.0 + nrm(ks[9], (DEPTH, D_MODEL), 0.05),
        "w_up": nrm(ks[10], (DEPTH, D_MODEL, D_FF), D_MODEL ** -0.5),
        "w_down": nrm(ks[11], (DEPTH, D_FF, D_MODEL), D_FF ** -0.5),
        "final_norm_g": 1.0 + nrm(ks[12], (D_MODEL,), 0.05),
    }

def reference(x, attn_norm_g, w_in, conv_w, w_conv_out, attn_sinks, rel_bias, w_attn_out, w_o,
              mlp_norm_g, w_up, w_down, final_norm_g):
    b, t, _ = x.shape
    for l in range(DEPTH):
        h = rmsnorm(x, attn_norm_g[l])
        proj = h @ w_in[l]
        u_b, u_c, u_x, q, k, v, g_conv, g_attn = jnp.split(proj, SPLITS, axis=-1)

        y_conv = (u_b * short_conv(u_c * u_x, conv_w[l])) @ w_conv_out[l]

        attn = sliding_window_attention(
            q.reshape(b, t, N_HEADS, HEAD_DIM),
            k.reshape(b, t, N_KV_HEADS, HEAD_DIM),
            v.reshape(b, t, N_KV_HEADS, HEAD_DIM),
            attn_sinks[l], rel_bias)
        y_attn = attn @ w_attn_out[l]

        mixed = jax.nn.sigmoid(g_conv) * y_conv + jax.nn.sigmoid(g_attn) * y_attn
        x = x + mixed @ w_o[l]

        h2 = rmsnorm(x, mlp_norm_g[l])
        x = x + jnp.square(jax.nn.relu(h2 @ w_up[l])) @ w_down[l]
    return rmsnorm(x, final_norm_g)


_drawn_inputs = setup_inputs


def setup_inputs(seed=0):
    import zlib

    import numpy as np

    out = dict(_drawn_inputs(seed))
    spreads = {}
    factors = {'attn_sinks': 8.0}
    for name, (base, spread) in spreads.items():
        noise = np.random.default_rng([zlib.crc32(name.encode()), seed]).standard_normal(out[name].shape)
        drawn = base * np.exp(spread * noise) if base else spread * noise
        out[name] = __import__('jax').numpy.asarray(drawn.astype(out[name].dtype))
    for name, factor in factors.items():
        out[name] = (out[name] * factor).astype(out[name].dtype)
    return out
```

```python
from contextlib import ExitStack

import numpy as np

import concourse.bass as bass
from concourse import mybir

F32 = mybir.dt.float32
F32R = mybir.dt.float32r
ALU = mybir.AluOpType
ACT = mybir.ActivationFunctionType

P = 128
D = 1024
T = 512
KT = D // P
TB = T // P
HEADS, KV, HD = 16, 2, 64
QUADS = 4
WINDOW, BUCKETS, MAX_DIST = 128, 32, 128
FF = 4 * D
EPS, NEG = 1e-6, -1e30
SCALE = HD ** -0.5

COL_B, COL_C, COL_X, COL_Q = 0, D, 2 * D, 3 * D
COL_KV = 4 * D
COL_GC = COL_KV + 2 * KV * HD
COL_GA = COL_GC + D

SC = 256
S_KV, S_Q = 0, 1
S_MIX = S_Q + 4
S_OUT = S_MIX + 3 * 4
S_WO = S_OUT + 4 * 4
S_MLP = S_WO + 4
STRIPS = S_MLP + 8 * 4


def t5_bucket(dist):
    n = np.maximum(dist, 0)
    exact = BUCKETS // 2
    ratio = np.log(np.maximum(n, exact).astype(np.float32) / exact) / np.log(MAX_DIST / exact)
    large = np.minimum(exact + (ratio * (BUCKETS - exact)).astype(np.int32), BUCKETS - 1)
    return np.where(n < exact, n, large)


def weight_slot(s):
    if s < S_MIX:
        return 0 if s == S_KV else (1, 2)[(s - S_Q) % 2]
    if s < S_OUT:
        return (1, 0, 2)[(s - S_MIX) % 3]
    return (1, 0, 2, 0)[(s - S_OUT) % 4]


def raw_slot(c):
    if c < 2 * S_Q:
        return 2 + c
    if c < 2 * S_MIX:
        return (c - 2 * S_Q) % 4
    if c < 2 * S_OUT:
        return (c - 2 * S_MIX) % 3
    return (0, 1, 3, 2)[(c - 2 * S_OUT) % 4]


def raw_uses(c):
    return sum(raw_slot(x) == raw_slot(c) for x in range(c + 1))


def raw_back(c):
    return next((d for d in range(1, c + 1) if raw_slot(c - d) == raw_slot(c)), None)


KINDS = (["kv"] + ["q"] * 4 + ["c", "x", "b"] * 4 + ["gc", "co", "ga", "ao"] * 4 + ["up"] * 16)
FREES = {"kv": "DA", "q": "DA", "c": "AA", "x": "DD", "b": "DD", "gc": "AA", "co": "DD", "ga": "AA",
         "ao": "DD", "up": "AA"}


def row_matrix(s):
    if S_WO <= s < S_MLP:
        return 0
    return (s - S_MLP) // 8 + 1 if s >= S_MLP and (s - S_MLP) % 8 >= 4 else None


def transposed_before(s):
    return sum(row_matrix(x) is None for x in range(s))


def frees(engine, half, t):
    return sum(FREES[KINDS[x]][half] == engine for x in range(t + 1))


class Pass:

    def __init__(self, reg, first, end):
        self.reg, self.first, self.end = reg, first, end


def at(f, x, step, it):
    if isinstance(it, int):
        return f(x + step * it)
    v = [f(x + step * i) for i in range(it.first, it.end)]
    slope = v[1] - v[0]
    assert all(b - a == slope for a, b in zip(v, v[1:]))
    return it.reg * slope + (v[0] - slope * it.first)


def index(it):
    return it if isinstance(it, int) else it.reg


def first_of(it):
    return it if isinstance(it, int) else it.first


def build(nc, x, attn_norm_g, w_in, conv_w, w_conv_out, attn_sinks, rel_bias, w_attn_out, w_o,
          mlp_norm_g, w_up, w_down, final_norm_g, out):
    ctx = ExitStack()
    with ctx:
        base = -(-nc.sbuf_base // 64) * 64
        top = [base]

        def place(name, shape, dt=F32, offset=None):
            size = 4 * int(np.prod(shape[1:]))
            if offset is None:
                offset = top[0]
                top[0] = -(-(offset + size) // 64) * 64
            return nc.alloc_sbuf_tensor_at(name, shape, dt, offset=offset)

        raw = [place(f"raw{i}", [P, 1024]) for i in range(4)]
        wgt = [place(f"wgt{i}", [P, 2, 2048], F32R) for i in range(3)]
        h = place("h", [P, 2, KT, T], F32R)
        qa_at = top[0]
        qa = place("qa", [P, KT, T])
        y = place("y", [P, KT, T])
        mix = place("mix", [P, 2, KT, T], F32R, offset=qa_at)
        hid = place("hid", [P, 2, KT, T], F32R, offset=qa_at)
        one_at = top[0]
        bias = place("bias", [P, HEADS, 2 * P])
        qs = place("qs", [P, KT, 2, P], F32R)
        khi = place("khi", [P, KV, P + T], F32R)
        vnat = place("vnat", [P, TB + 1, KV * HD])
        xn = place("xn", [P, TB, D], offset=one_at)
        ysplit = place("ysplit", [P, 2, KT, T], F32R, offset=one_at)
        top[0] = max(top[0], one_at + 4 * 2 * KT * T)
        two_at = top[0]
        klo = place("klo", [P, KV, P + T], F32R)
        pr = place("pr", [P, 2, 4, 2 * P])
        pt = place("pt", [P, 2, 2, 4 * P], F32R)
        vs = place("vs", [P, 2, 2, KV, 3 * HD], F32R)
        asplit = place("asplit", [P, 2, KT, T], F32R, offset=two_at)
        res = place("res", [P, TB, D], offset=two_at)
        gfin = place("gfin", [P, D], offset=two_at + 4 * TB * D)
        top[0] = max(top[0], two_at + 4 * 2 * KT * T)
        ta = place("ta", [P, 2, T])
        tz = place("tz", [P, 2, T + 2])
        ty = place("ty", [P, 2, T])
        ident = place("ident", [P, P])
        prow = place("prow", [5 * KT, P])
        pcol = place("pcol", [P, 5 * KT])
        rbt = place("rbt", [HEADS, BUCKETS])
        ext = place("ext", [HEADS, 3 * P])
        sink = place("sink", [P, HEADS])
        eps = place("eps", [P, 1])
        ssq = place("ssq", [P, TB])
        rms = place("rms", [P, 2, TB])
        ss2 = place("ss2", [P, TB])
        rr2 = place("rr2", [P, 2, TB])
        ss3 = place("ss3", [P, 2, TB])
        rms3 = place("rms3", [P, 3, TB])
        top_m = place("top_m", [P, 2, 4])
        neg_m = place("neg_m", [P, 2, 4])
        snk_d = place("snk_d", [P, 2, 4])
        den = place("den", [P, 2, 4])
        tot = place("tot", [P, 2, 4])
        rec = place("rec", [P, 2, 4])
        g1, g2 = 0, KT
        bias_rows = nc.dram_tensor("bias_rows", (HEADS, 3 * P), F32)

        bank = [ctx.enter_context(nc.psum_tensor(f"bank{i}", [P, T], F32)) for i in range(8)]
        B_SC, B_PT, B_PV, B_VT = 2, 4, 6, 7

        def sem(name):
            return ctx.enter_context(nc.semaphore(name))

        x_in = [sem(f"x_in{b}") for b in range(TB)]
        raw_in = [sem(f"raw_in{i}") for i in range(4)]
        rows_in, table_in, bias_out, bias_in, res_in, out_done = (
            sem(n) for n in ("rows_in", "table_in", "bias_out", "bias_in", "res_in", "out_done"))
        hi_ready, lo_ready, row_part = sem("hi_ready"), sem("lo_ready"), sem("row_part")
        half_ready = [sem(f"half_ready{j}") for j in range(2)]
        free_act = [sem(f"free_act{j}") for j in range(2)]
        free_dve = [sem(f"free_dve{j}") for j in range(2)]
        ident_step, zeroed, ext_step = sem("ident_step"), sem("zeroed"), sem("ext_step")
        par_t, par_ready = sem("par_t"), sem("par_ready")
        sq_done, rms_step, xn_ready, xt_ready = sem("sq_done"), sem("rms_step"), sem("xn_ready"), sem("xt_ready")
        h_hi, h_ready = sem("h_hi"), sem("h_ready")
        k_hi, vt_done, v_ready, conv1 = sem("k_hi"), sem("vt_done"), sem("v_ready"), sem("conv1")
        qs_hi, qs_ready, vs_hi, vs_ready = sem("qs_hi"), sem("qs_ready"), sem("vs_hi"), sem("vs_ready")
        qk_ready, logits, shift_ready, exp_ready = (sem(n) for n in
                                                    ("qk_ready", "logits", "shift_ready", "exp_ready"))
        tot_ready, rec_ready, p_ready = sem("tot_ready"), sem("rec_ready"), sem("p_ready")
        t_ready, pt_hi, pt_ready, pv_ready, pv_out = (sem(n) for n in
                                                      ("t_ready", "pt_hi", "pt_ready", "pv_ready", "pv_out"))
        sp_hi, sp_ready = sem("sp_hi"), sem("sp_ready")
        mix_f, mix_hi, mix_ready = sem("mix_f"), sem("mix_hi"), sem("mix_ready")
        row_ready, row_free = sem("row_ready"), sem("row_free")
        rt_ready, h2_hi, h2_ready = sem("rt_ready"), sem("h2_hi"), sem("h2_ready")
        ss2_ready, rr2_step = sem("ss2_ready"), sem("rr2_step")
        sqr, hid_hi, hid_ready = sem("sqr"), sem("hid_hi"), sem("hid_ready")
        passed = sem("passed")
        root_done, root3_part, root3_done = sem("root_done"), sem("root3_part"), sem("root3_done")
        ss3_ready, gained, fin_step = sem("ss3_ready"), sem("gained"), sem("fin_step")
        out_left, out_right = sem("out_left"), sem("out_right")

        def wait(eng, s, value):
            if not isinstance(value, int) or value > 0:
                eng.wait_ge(s, value)

        def wait_apart(eng, s, value):
            wait(eng, s, value)
            if not isinstance(value, int):
                eng.sem_inc(passed, 1)

        def f32(ap):
            return ap.bitcast(F32)

        def cols(start, size):
            return bass.ds(start, size)

        block = ctx.enter_context(nc.Block())

        @block.sync
        def _(sp):
            def load_chunk(c, step, it, src):
                its = [it] if isinstance(it, int) else range(it.first, it.end)
                backs = [raw_back(c + step * i) for i in its]
                n = raw_slot(c + step * first_of(it))
                assert all(raw_slot(c + step * i) == n for i in its)
                if backs[0] is not None:
                    wait_apart(sp, lo_ready, at(lambda v: v - min(backs) + 1, c, step, it))
                dst = raw[n][:, :].rearrange("p (k n) -> p k n", k=src.shape[1])
                sp.dma_start(dst, src).then_inc(raw_in[n], 16)

            def load_t(s, step, it, w, col):
                v = w.rearrange("(k p) n -> p k n", p=P)
                for a in range(2):
                    load_chunk(2 * s + a, 2 * step, it, v[:, 4 * a:4 * a + 4, cols(col, SC)])

            def load_row(s, step, it, w, row_tile, col):
                v = w.rearrange("(k p) n -> p k n", p=P)
                for a in range(2):
                    load_chunk(2 * s + a, 2 * step, it, v[:, cols(row_tile + 2 * a, 2), col:col + 512])

            for b in range(TB):
                sp.dma_start(xn[:, b, :], x[b * P:(b + 1) * P, :]).then_inc(x_in[b], 16)
            load_t(S_KV, 0, 0, w_in, COL_KV)
            load_t(S_Q, 0, 0, w_in, COL_Q)
            sp.wait_ge(ext_step, 1 + BUCKETS)
            sp.dma_start(bias_rows[:, :], ext[:, :]).then_inc(bias_out, 16)
            sp.wait_ge(bias_out, 16)
            sp.wait_ge(xt_ready, TB)
            band = bass.AP(bias_rows, 0, [[1, P], [3 * P, HEADS], [1, 2 * P]])
            sp.dma_start(bias[:, :, :], band).then_inc(bias_in, 16)
            for i in range(1, 4):
                load_t(S_Q + i, 0, 0, w_in, COL_Q + SC * i)
            with sp.Fori(0, 4) as n:
                it = Pass(n, 0, 4)
                load_t(S_MIX, 3, it, w_in, n * SC + COL_C)
                load_t(S_MIX + 1, 3, it, w_in, n * SC + COL_X)
                load_t(S_MIX + 2, 3, it, w_in, n * SC + COL_B)
            with sp.Fori(0, 4) as n:
                it = Pass(n, 0, 4)
                load_t(S_OUT, 4, it, w_in, n * SC + COL_GC)
                load_t(S_OUT + 1, 4, it, w_conv_out, n * SC)
                load_t(S_OUT + 2, 4, it, w_in, n * SC + COL_GA)
                load_t(S_OUT + 3, 4, it, w_attn_out, n * SC)
            for i in range(4):
                load_row(S_WO + i, 0, 0, w_o, 4 * (i % 2), 512 * (i // 2))
            with sp.Fori(0, 4) as i:
                it = Pass(i, 0, 4)
                for u in range(4):
                    load_t(S_MLP + u, 8, it, w_up, i * D + SC * u)
                for u in range(4):
                    load_row(S_MLP + 4 + u, 8, it, w_down, i * KT + 4 * (u % 2), 512 * (u // 2))
            for b in range(TB):
                for ch in range(2):
                    sp.wait_ge((out_left, out_right)[ch], b + 1)
                    sp.dma_start(out[b * P:(b + 1) * P, 512 * ch:512 * ch + 512],
                                 res[:, b, 512 * ch:512 * ch + 512]).then_inc(out_done, 16)
            sp.wait_ge(out_done, 16 * 2 * TB)

        @block.gpsimd
        def _(pool):
            g = nc.gpsimd
            g.memset(ident[:, :], 0.0).then_inc(ident_step, 1)
            g.memset(eps[:, :], EPS).then_inc(ident_step, 1)
            pool.wait_ge(ident_step, 2)
            g.affine_select(out=ident[:, :], in_=ident[:, :], compare_op=ALU.not_equal, fill=1.0, base=0,
                            pattern=[[-1, P]], channel_multiplier=1).then_inc(ident_step, 1)
            with nc.allow_non_contiguous_dma("a table of 32 x 16"):
                pool.dma_start(rbt[:, :], rel_bias.rearrange("b h -> h b")).then_inc(table_in, 16)
            pool.dma_start(sink[:, :], bass.AP(attn_sinks.tensor, 0, [[0, P], [1, HEADS]])).then_inc(table_in, 16)
            g.memset(ext[:, :], NEG).then_inc(ext_step, 1)
            pool.wait_ge(table_in, 16 * 2)
            pool.wait_ge(ext_step, 1)
            bucket = t5_bucket(np.arange(WINDOW))
            for b in range(BUCKETS):
                dist = np.flatnonzero(bucket == b)
                m0, n = 2 * P - 1 - int(dist[-1]), len(dist)
                g.tensor_copy(ext[:, m0:m0 + n], rbt[:, b:b + 1].to_broadcast([HEADS, n])).then_inc(ext_step, 1)
            for t in (f32(khi[:, :, 0:P]), f32(klo[:, :, 0:P]), pr[:, :, :, 0:P], vnat[:, 0, :],
                      f32(vs[:, 0, :, :, :]), f32(vs[:, 1, :, :, :]), tz[:, :, 0:2]):
                g.memset(t, 0.0).then_inc(zeroed, 1)
        N_ZEROED = 7

        @block.tensor
        def _(pe):
            mm = nc.tensor.matmul

            def transposed_strip(s, step, it, t, tstep, rhs, hooks={}, k_wait=None,
                                 bank_wait=None, by_chunk=False):
                first = first_of(it)
                w = wgt[weight_slot(s + step * first)][:, :, :].rearrange("p c (k n) -> p c k n", k=KT)
                quarters = [(j, e) for j in range(2) for e in range(2)]
                if by_chunk:
                    quarters = [(j, e) for e, j in quarters]
                for q, (j, e) in enumerate(quarters):
                    if e == 0 and t + tstep * first > 0:
                        who = FREES[KINDS[t - 1 + tstep * first]][j]
                        wait(pe, (free_act if who == "A" else free_dve)[j],
                             at(lambda v: frees(who, j, v), t - 1, tstep, it))
                    if e == 0 and bank_wait:
                        bank_wait(j)
                    if j == 0:
                        wait(pe, lo_ready, at(lambda v: 2 * v + e + 1, s, step, it))
                    for k in range(4 * e, 4 * e + 4):
                        if j == 0 and k_wait:
                            k_wait(k)
                        wh = w[:, 0, k, j * P:(j + 1) * P]
                        wl = w[:, 1, k, j * P:(j + 1) * P]
                        mm(bank[j][:, :], wh, rhs[:, 0, k, :], start=(k == 0), stop=False)
                        mm(bank[j][:, :], wh, rhs[:, 1, k, :], start=False, stop=False)
                        last = mm(bank[j][:, :], wl, rhs[:, 0, k, :], start=False, stop=(k == KT - 1))
                    if e == 1:
                        last.then_inc(half_ready[j], 1)
                    for f in hooks.get(q, ()):
                        f()

            def row_strip(s, step, it, m, ch, kh, lhs, k_wait=None, hooks={}):
                w = wgt[weight_slot(s + step * first_of(it))][:, :, :].rearrange("p c (k n) -> p c k n", k=4)
                for b in range(TB):
                    acc = bank[4 + b if ch == 0 else b]
                    if kh == 0 and (not isinstance(m, int) or m > 0):
                        wait(pe, row_free, 8 * (m - 1) + (4 * ch + b + 1))
                    for kk in range(4):
                        k = 4 * kh + kk
                        if b == 0 and kk % 2 == 0:
                            wait(pe, lo_ready, at(lambda v: 2 * v + kk // 2 + 1, s, step, it))
                        if b == 0 and k_wait:
                            k_wait(k)
                        lh = lhs[:, 0, k, b * P:(b + 1) * P]
                        ll = lhs[:, 1, k, b * P:(b + 1) * P]
                        mm(acc[:, :], lh, w[:, 0, kk, :], start=(k == 0), stop=False)
                        mm(acc[:, :], ll, w[:, 0, kk, :], start=False, stop=False)
                        last = mm(acc[:, :], lh, w[:, 1, kk, :], start=False, stop=(k == KT - 1))
                        if k == KT - 1:
                            last.then_inc(row_ready, 1)
                        elif kk == 3 and b == TB - 1:
                            last.then_inc(row_part, 1)
                    for f in hooks.get(b, ()):
                        f()

            def scores(n, qd):
                if qd == 0:
                    pe.wait_ge(free_dve[0], 1)
                    pe.wait_ge(zeroed, N_ZEROED)
                    wait(pe, qs_ready, 2 * n + 2)
                wait(pe, logits, 4 * n + qd)
                for i in range(4):
                    head = 4 * qd + i
                    acc = bank[B_SC + i // 2][:, 256 * (i % 2):256 * (i % 2) + 256]
                    q = qs[:, head // 2, head % 2, :]
                    kg = head // (HEADS // KV)
                    mm(acc, q, khi[:, kg, cols(n * P, 2 * P)], start=True, stop=False)
                    last = mm(acc, q, klo[:, kg, cols(n * P, 2 * P)], start=False, stop=True)
                last.then_inc(qk_ready, 1)

            def transpose_probs(n, qd):
                wait(pe, p_ready, 4 * n + (qd + 1))
                wait(pe, pt_ready, 8 * n + 2 * qd)
                for kb in range(2):
                    for i in range(4):
                        c = 2 * (i % 2) + i // 2
                        last = nc.tensor.transpose(bank[B_PT + kb][:, c * P:(c + 1) * P],
                                                   pr[:, qd % 2, i, kb * P:(kb + 1) * P], ident[:, :])
                    last.then_inc(t_ready, 1)

            def values(n, qd):
                wait(pe, pt_ready, 8 * n + (2 * qd + 2))
                if qd == 0:
                    wait(pe, vs_ready, n + 1)
                wait(pe, pv_out, 4 * n + qd)
                kg = qd // 2
                steps = [(kb, par, vp, pp) for kb in range(2) for par in range(2)
                         for vp, pp in ((0, 0), (1, 0), (0, 1))]
                for e, (kb, par, vp, pp) in enumerate(steps):
                    v = vs[:, vp, kb, kg, HD:3 * HD] if par == 0 else vs[:, vp, kb, kg, 0:2 * HD]
                    last = mm(bank[B_PV][:, 0:256], v, pt[:, pp, kb, 256 * par:256 * par + 256],
                              start=(e == 0), stop=(e == len(steps) - 1))
                last.then_inc(pv_ready, 1)

            def x_transpose(b, k):
                return nc.tensor.transpose(bank[k][:, b * P:(b + 1) * P], xn[:, b, k * P:(k + 1) * P], ident[:, :])

            pe.wait_ge(ident_step, 3)
            for b in range(TB):
                pe.wait_ge(xn_ready, b + 1)
                for k in range(KT - 1):
                    x_transpose(b, k)
                if b == 0:
                    pe.wait_ge(rows_in, 16 * 3)
                    nc.tensor.transpose(bank[KT - 1][:, 0:5 * KT], prow[:, :],
                                        ident[0:5 * KT, 0:5 * KT]).then_inc(par_t, 1)
                    continue
                if b == 1:
                    pe.wait_ge(par_ready, 1)
                    x_transpose(0, KT - 1).then_inc(xt_ready, 1)
                x_transpose(b, KT - 1).then_inc(xt_ready, 1)

            def first_tile(k):
                pe.wait_ge(h_ready, k + 1)

            transposed_strip(S_KV, 0, 0, 0, 0, h, k_wait=first_tile)

            def value_transposes():
                pe.wait_ge(free_act[1], 1)
                for b in range(TB):
                    last = nc.tensor.transpose(bank[B_VT][:, b * P:(b + 1) * P], ty[:, 1, b * P:(b + 1) * P],
                                               ident[:, :])
                last.then_inc(vt_done, 1)

            with pe.Fori(0, 2) as i:
                it = Pass(i, 0, 2)
                transposed_strip(S_Q, 2, it, 1, 2, h)
                transposed_strip(S_Q + 1, 2, it, 2, 2, h)
            value_transposes()

            def mixer_block(n, it, before):
                def on(f, m, qd):
                    return lambda: f(m, qd)
                prev = before is not None
                transposed_strip(S_MIX, 3, it, 5, 3, h, hooks={
                    1: ([on(values, before, 2)] if prev else []) + [on(scores, n, 0)],
                    2: [on(transpose_probs, before, 3)] if prev else []})
                transposed_strip(S_MIX + 1, 3, it, 6, 3, h, hooks={
                    0: ([on(values, before, 3)] if prev else []) + [on(scores, n, 1)],
                    2: [on(transpose_probs, n, 0)],
                    3: [on(scores, n, 2)]})
                transposed_strip(S_MIX + 2, 3, it, 7, 3, h, hooks={
                    0: [on(values, n, 0)],
                    1: [on(transpose_probs, n, 1)],
                    2: [on(scores, n, 3)],
                    3: [on(values, n, 1), on(transpose_probs, n, 2)]})

            mixer_block(0, 0, None)
            with pe.Fori(1, TB) as n:
                mixer_block(n, Pass(n, 1, TB), n - 1)

            def branch_group(it, hooks={}):
                transposed_strip(S_OUT, 4, it, 17, 4, h, hooks=hooks)
                transposed_strip(S_OUT + 1, 4, it, 18, 4, ysplit,
                                 k_wait=lambda k: pe.wait_ge(sp_ready, k // 4 + 1) if k % 4 == 0 else None)
                transposed_strip(S_OUT + 2, 4, it, 19, 4, h)
                transposed_strip(S_OUT + 3, 4, it, 20, 4, asplit,
                                 k_wait=lambda k: pe.wait_ge(sp_ready, k // 4 + 3) if k % 4 == 0 else None)

            branch_group(0, {1: [lambda: values(3, 2), lambda: transpose_probs(3, 3)], 3: [lambda: values(3, 3)]})
            with pe.Fori(1, 4) as j:
                branch_group(Pass(j, 1, 4))

            def residual_transposes(b, ch):
                pe.wait_ge(row_free, 4 * ch + b + 1)
                if ch == 0 and b == 0:
                    pe.wait_ge(row_free, TB)
                if ch == 1 and b == 0:
                    pe.wait_ge(h2_ready, 4)
                for f in range(4):
                    last = nc.tensor.transpose(bank[4 + f][:, b * P:(b + 1) * P],
                                               res[:, b, 512 * ch + f * P:512 * ch + (f + 1) * P], ident[:, :])
                last.then_inc(rt_ready, 1)

            def rt(b, ch):
                return lambda: residual_transposes(b, ch)

            row_strip(S_WO, 0, 0, 0, 0, 0, mix, k_wait=lambda k: pe.wait_ge(mix_ready, k + 1))
            row_strip(S_WO + 1, 0, 0, 0, 0, 1, mix, k_wait=lambda k: pe.wait_ge(mix_ready, k + 1))
            row_strip(S_WO + 2, 0, 0, 0, 1, 0, mix, hooks={1: [rt(0, 0), rt(1, 0)], 2: [rt(2, 0), rt(3, 0)]})
            row_strip(S_WO + 3, 0, 0, 0, 1, 1, mix, hooks={1: [rt(0, 1)], 2: [rt(1, 1)], 3: [rt(2, 1)]})

            def mlp_quarter(it, hooks={}):
                for u in range(4):
                    transposed_strip(S_MLP + u, 8, it, 33 + u, 4, h, hooks=hooks if u == 0 else {},
                                     by_chunk=isinstance(it, int) and u == 0,
                                     k_wait=lambda k: pe.wait_ge(h2_ready, k + 1) if u == 0 else None,
                                     bank_wait=lambda j: pe.wait_ge(row_free, index(it) * 8 + (5 + j))
                                     if u == 0 else None)
                for u in range(4):
                    row_strip(S_MLP + 4 + u, 8, it, index(it) + 1, u // 2, u % 2, hid,
                              k_wait=lambda k: pe.wait_ge(hid_ready, index(it) * 8 + (k + 1)) if u < 2 else None)

            mlp_quarter(0, {0: [rt(3, 1)]})
            with pe.Fori(1, 4) as i:
                mlp_quarter(Pass(i, 1, 4))

        @block.scalar
        def _(act):
            a = nc.scalar.activation

            def slot_free(s, step, it):
                s1 = s + step * first_of(it)
                if s1 < 0:
                    return
                m = row_matrix(s1)
                if m is None:
                    wait(act, half_ready[1], at(lambda v: transposed_before(v) + 1, s, step, it))
                elif (s1 - S_WO) % 2 == 0:
                    wait(act, row_part, at(lambda v: 2 * row_matrix(v) + (v - S_WO) % 4 // 2 + 1, s, step, it))
                else:
                    wait(act, row_ready, at(lambda v: 8 * row_matrix(v) + 4 * ((v - S_WO) % 4 // 2) + 4, s, step, it))

            def hi_chunks(s, step=0, it=0):
                s1 = s + step * first_of(it)
                for e in range(2):
                    c, c1 = 2 * s + e, 2 * s1 + e
                    wait(act, raw_in[raw_slot(c1)], at(lambda v: 16 * raw_uses(v), c, 2 * step, it))
                    if e == 0:
                        slot_free(s - 2, step, it)
                    a(wgt[weight_slot(s1)][:, 0, 1024 * e:1024 * e + 1024], raw[raw_slot(c1)][:, :],
                      ACT.Copy).then_inc(hi_ready, 1)

            act.dma_start(prow[0:KT, :], attn_norm_g.rearrange("a (k p) -> (a k) p", p=P)).then_inc(rows_in, 16)
            act.dma_start(prow[KT:2 * KT, :], mlp_norm_g.rearrange("a (k p) -> (a k) p", p=P)).then_inc(rows_in, 16)
            act.dma_start(prow[2 * KT:5 * KT, :], conv_w.rearrange("a t (k p) -> (a t k) p", p=P)).then_inc(rows_in, 16)
            scratch = tz[:, :, :].rearrange("p a n -> p (a n)")[:, 0:D]
            act.wait_ge(ident_step, 2)
            a(rms[:, 0, 0:1], eps[:, :], ACT.Sqrt)
            for b in range(TB):
                act.wait_ge(x_in[b], 16)
                a(ta[:, :, :].rearrange("p a n -> p (a n)"), xn[:, b, :], ACT.Square, accum_out=ssq[:, b:b + 1]).then_inc(sq_done, 1)
                act.wait_ge(sq_done, b + 1)
                a(rms[:, 0, b:b + 1], ssq[:, b:b + 1], ACT.Sqrt, bias=eps[:, :], scale=1.0 / D).then_inc(root_done, 1)
            hi_chunks(S_KV)
            act.wait_ge(par_ready, 1)
            act.wait_ge(xt_ready, TB)
            for k in range(KT):
                a(h[:, 0, k, :], bank[k][:, :], ACT.Copy, scale=pcol[:, g1 + k:g1 + k + 1]).then_inc(h_hi, 1)
            hi_chunks(S_Q)
            act.wait_ge(half_ready[0], 1)
            for kg in range(KV):
                for up in range(2):
                    a(khi[HD * up:HD * up + HD, kg, P:P + T], bank[0][HD * kg:HD * kg + HD, :], ACT.Copy,
                      scale=SCALE).then_inc(k_hi, 1)
            act.wait_ge(half_ready[1], 1)
            a(ty[:, 1, :], bank[1][:, :], ACT.Copy).then_inc(free_act[1], 1)
            with act.Fori(0, 2) as i:
                for e in range(2):
                    hi_chunks(S_Q + 1 + e, 2, Pass(i, 0, 2))
                    act.wait_ge(half_ready[1], i * 2 + (2 + e))
                    a(qa[:, cols(i * 4 + (2 * e + 1), 1), :], bank[1][:, :].rearrange("p (a n) -> p a n", a=1),
                      ACT.Copy).then_inc(free_act[1], 1)

            def stage_queries(n):
                wait(act, qk_ready, 4 * n)
                act.wait_ge(free_dve[0], frees("D", 0, S_MIX - 1))
                act.wait_ge(free_act[1], frees("A", 1, S_MIX - 1))
                for par in range(2):
                    half = slice(HD * par, HD * par + HD)
                    a(qs[half, :, par, ::-1], qa[half, :, cols(n * P, P)], ACT.Copy).then_inc(qs_hi, 1)

            def stage_values(n):
                if isinstance(n, int):
                    act.wait_ge(v_ready, 1)
                    act.wait_ge(zeroed, N_ZEROED)
                wait(act, pv_ready, 4 * n)
                a(vs[:, 0, :, :, HD:2 * HD], vnat[:, cols(n, 2), :].rearrange("p b (g d) -> p b g d", g=KV),
                  ACT.Copy).then_inc(vs_hi, 1)

            def exponentials(n, qd, first):
                wait(act, shift_ready, 4 * n + (qd + 1))
                lo = P if first else 0
                for i in range(4):
                    v = pr[:, qd % 2, i, lo:2 * P]
                    a(v, v, ACT.Exp, bias=neg_m[:, qd % 2, i:i + 1], accum_out=den[:, qd % 2, i:i + 1])
                a(snk_d[:, qd % 2, :], snk_d[:, qd % 2, :], ACT.Exp).then_inc(exp_ready, 1)

            def probs_hi(n, qd):
                wait(act, pv_ready, 4 * n + qd)
                for kb in range(2):
                    wait(act, t_ready, 8 * n + (2 * qd + kb + 1))
                    a(pt[:, 0, kb, :], bank[B_PT + kb][:, :], ACT.Copy).then_inc(pt_hi, 1)

            def mixer_block(n, it, before):
                if before is not None:
                    probs_hi(before, 2)
                stage_queries(n)
                hi_chunks(S_MIX + 1, 3, it)
                for j in range(2):
                    act.wait_ge(half_ready[j], at(lambda v: v + 1, 5, 3, it))
                    a(ta[:, j, :], bank[j][:, :], ACT.Copy).then_inc(free_act[j], 1)
                    if j == 0 and before is not None:
                        probs_hi(before, 3)
                hi_chunks(S_MIX + 2, 3, it)
                exponentials(n, 0, before is None)
                stage_values(n)
                exponentials(n, 1, before is None)
                probs_hi(n, 0)
                hi_chunks(S_MIX + 3, 3, it)
                exponentials(n, 2, before is None)
                probs_hi(n, 1)
                exponentials(n, 3, before is None)

            mixer_block(0, 0, None)
            with act.Fori(1, TB) as n:
                mixer_block(n, Pass(n, 1, TB), n - 1)

            def split(dst, src, e):
                a(dst[:, 0, 4 * e:4 * e + 4, :], src[:, 4 * e:4 * e + 4, :], ACT.Copy).then_inc(sp_hi, 1)

            def gate(j, t, it):
                used = at(lambda v: frees("D", j, v - 1), t, 4, it)
                act.wait_ge(half_ready[j], at(lambda v: v + 1, t, 4, it))
                act.wait_ge(free_dve[j], used)
                a(ta[:, j, :], bank[j][:, :], ACT.Sigmoid).then_inc(free_act[j], 1)

            def branch_group(it, first):
                if first:
                    probs_hi(3, 2)
                hi_chunks(S_OUT + 1, 4, it)
                if first:
                    act.wait_ge(free_dve[1], frees("D", 1, 16))
                    act.wait_ge(vs_ready, TB)
                    act.wait_ge(logits, QUADS * TB)
                    split(ysplit, y, 0)
                gate(0, 17, it)
                if first:
                    probs_hi(3, 3)
                    split(ysplit, y, 1)
                gate(1, 17, it)
                hi_chunks(S_OUT + 2, 4, it)
                if first:
                    act.wait_ge(pv_out, QUADS * TB)
                    split(asplit, qa, 0)
                    split(asplit, qa, 1)
                hi_chunks(S_OUT + 3, 4, it)
                gate(0, 19, it)
                gate(1, 19, it)
                hi_chunks(S_OUT + 4, 4, it)
                for j in range(2):
                    act.wait_ge(mix_f, index(it) * 2 + (j + 1))
                    a(mix[:, 0, cols(index(it) * 2 + j, 1), :], ty[:, j:j + 1, :], ACT.Copy).then_inc(mix_hi, 1)

            branch_group(0, True)
            with act.Fori(1, 4) as j:
                branch_group(Pass(j, 1, 4), False)

            a(rms3[:, 1, 0:1], eps[:, :], ACT.Sqrt)

            def norm_hi(ch):
                act.wait_ge(rt_ready, TB * (ch + 1))
                for f in range(4):
                    k = 4 * ch + f
                    a(h[:, 0, k, :], bank[4 + f][:, :], ACT.Copy, scale=pcol[:, g2 + k:g2 + k + 1]).then_inc(h2_hi, 1)

            hi_chunks(S_WO + 1)
            act.wait_ge(half_ready[1], transposed_before(S_WO))
            act.dma_start(res[:, :, :], x.rearrange("(b p) n -> p b n", p=P)).then_inc(res_in, 16)
            act.dma_start(gfin[:, :], bass.AP(final_norm_g.tensor, 0, [[0, P], [1, D]])).then_inc(res_in, 16)
            hi_chunks(S_WO + 2)
            hi_chunks(S_WO + 3)
            norm_hi(0)
            hi_chunks(S_MLP)
            norm_hi(1)

            def mlp_quarter(it, first=False, last=False):
                for u in range(4):
                    hi_chunks(S_MLP + u + 1, 8, it)
                    for j in range(2):
                        act.wait_ge(half_ready[j], at(lambda v: v + 1, 33 + u, 4, it))
                        a(ta[:, j, :], bank[j][:, :], ACT.Relu).then_inc(free_act[j], 1)
                        act.wait_ge(sqr, index(it) * 8 + (2 * u + j + 1))
                        a(hid[:, 0, 2 * u + j, :], ty[:, j, :], ACT.Copy).then_inc(hid_hi, 1)
                    if first and u == 0:
                        for b in range(TB):
                            act.wait_ge(ss2_ready, b) if b else None
                            a(scratch, res[:, b, :], ACT.Square, accum_out=ss2[:, b:b + 1]).then_inc(ss2_ready, 1)
                for u in range(4):
                    if not (last and u == 3):
                        hi_chunks(S_MLP + u + 5, 8, it)
                    if last and u == 1:
                        for b in range(TB):
                            act.wait_ge(row_free, 8 * 4 + b + 1)
                            if b:
                                act.wait_ge(ss3_ready, b)
                            a(scratch[:, 0:512], res[:, b, 0:512], ACT.Square, accum_out=ss3[:, 0, b:b + 1]).then_inc(ss3_ready, 1)
                        act.wait_ge(ss3_ready, TB)
                        a(rms3[:, 0, :], ss3[:, 0, :], ACT.Identity, bias=eps[:, :], scale=1.0 / D).then_inc(root3_part, 1)
                    if last and u == 3:
                        act.wait_ge(root3_part, 1)
                        for b in range(TB):
                            act.wait_ge(row_free, 8 * 4 + 4 + b + 1)
                            act.wait_ge(ss3_ready, TB + b)
                            a(scratch[:, 0:512], res[:, b, 512:D], ACT.Square, accum_out=ss3[:, 1, b:b + 1]).then_inc(ss3_ready, 1)
                            act.wait_ge(ss3_ready, TB + b + 1)
                            a(rms3[:, 1, b:b + 1], ss3[:, 1, b:b + 1], ACT.Sqrt, bias=rms3[:, 0, b:b + 1],
                              scale=1.0 / D).then_inc(root3_done, 1)
                            act.wait_ge(gained, b + 1)
                            act.wait_ge(fin_step, b + 1)
                            a(res[:, b, 0:512], res[:, b, 0:512], ACT.Copy, scale=rms3[:, 2, b:b + 1]).then_inc(out_left, 1)

            mlp_quarter(0, first=True)
            with act.Fori(1, 3) as i:
                mlp_quarter(Pass(i, 1, 3))
            mlp_quarter(3, last=True)

        @block.vector
        def _(dve):
            v = nc.vector
            def lo_chunks(s, step=0, it=0):
                s1 = s + step * first_of(it)
                for e in range(2):
                    wait(dve, hi_ready, at(lambda w: 2 * w + e + 1, s, step, it))
                    w = wgt[weight_slot(s1)]
                    v.tensor_tensor(w[:, 1, 1024 * e:1024 * e + 1024], raw[raw_slot(2 * s1 + e)][:, :],
                                    f32(w[:, 0, 1024 * e:1024 * e + 1024]), ALU.subtract).then_inc(lo_ready, 1)

            for b in range(TB):
                dve.wait_ge(root_done, b + 1)
                v.reciprocal(rms[:, 1, b:b + 1], rms[:, 0, b:b + 1]).then_inc(rms_step, 1)
                dve.wait_ge(rms_step, b + 1)
                v.tensor_scalar(xn[:, b, :], xn[:, b, :], rms[:, 1, b:b + 1], None, ALU.mult).then_inc(xn_ready, 1)
                if b == 1:
                    dve.wait_ge(par_t, 1)
                    v.tensor_copy(pcol[:, :], bank[KT - 1][:, 0:5 * KT]).then_inc(par_ready, 1)
            lo_chunks(S_KV)
            for k in range(KT):
                dve.wait_ge(h_hi, k + 1)
                v.scalar_tensor_tensor(out=h[:, 1, k, :], in0=bank[k][:, :], scalar=pcol[:, g1 + k:g1 + k + 1],
                                       in1=f32(h[:, 0, k, :]), op0=ALU.mult, op1=ALU.subtract).then_inc(h_ready, 1)
            lo_chunks(S_Q)
            for kg in range(KV):
                src = slice(HD * kg, HD * kg + HD)
                dve.wait_ge(k_hi, 2 * kg + 2)
                for up in range(2):
                    i = v.scalar_tensor_tensor(out=klo[HD * up:HD * up + HD, kg, P:P + T], in0=bank[0][src, :],
                                               scalar=SCALE, in1=f32(khi[src, kg, P:P + T]), op0=ALU.mult,
                                               op1=ALU.subtract)
            i.then_inc(free_dve[0], 1)
            with dve.Fori(0, 2) as i:
                for e in range(2):
                    lo_chunks(S_Q + 1 + e, 2, Pass(i, 0, 2))
                    dve.wait_ge(half_ready[0], i * 2 + (2 + e))
                    v.tensor_copy(qa[:, cols(i * 4 + 2 * e, 1), :], bank[0][:, :].rearrange("p (a n) -> p a n", a=1)
                                  ).then_inc(free_dve[0], 1)
            dve.wait_ge(vt_done, 1)
            v.tensor_copy(vnat[:, 1:TB + 1, :], bank[B_VT][:, :].rearrange("p (b n) -> p b n", b=TB)).then_inc(v_ready, 1)

            def stage_queries(n):
                for par in range(2):
                    half, other = slice(HD * par, HD * par + HD), slice(HD - HD * par, 2 * HD - HD * par)
                    wait(dve, qs_hi, 2 * n + (par + 1))
                    v.tensor_tensor(qs[other, :, par, ::-1], qa[half, :, cols(n * P, P)], f32(qs[half, :, par, ::-1]),
                                    ALU.subtract).then_inc(qs_ready, 1)

            def stage_values(n):
                wait(dve, vs_hi, n + 1)
                for kb in range(2):
                    i = v.tensor_tensor(vs[:, 1, kb, :, HD:2 * HD],
                                        vnat[:, cols(n + kb, 1), :].rearrange("p b (g d) -> p (b g) d", g=KV),
                                        f32(vs[:, 0, kb, :, HD:2 * HD]), ALU.subtract)
                i.then_inc(vs_ready, 1)

            def add_bias(n, qd, first):
                wait_apart(dve, qk_ready, 4 * n + (qd + 1))
                lo = P if first else 0
                for i in range(4):
                    head = 4 * qd + i
                    i_ = v.tensor_tensor_reduce(
                        out=pr[:, qd % 2, i, lo:2 * P], in0=bank[B_SC + i // 2][:, 256 * (i % 2) + lo:256 * (i % 2) + 256],
                        in1=bias[:, head, lo:2 * P], scale=1.0, scalar=sink[:, head:head + 1], op0=ALU.add,
                        op1=ALU.max, accum_out=top_m[:, qd % 2, i:i + 1])
                i_.then_inc(logits, 1)
                wait(dve, logits, 4 * n + (qd + 1))
                v.tensor_scalar(neg_m[:, qd % 2, :], top_m[:, qd % 2, :], -1.0, None, ALU.mult)
                v.tensor_tensor(snk_d[:, qd % 2, :], sink[:, 4 * qd:4 * qd + 4], top_m[:, qd % 2, :],
                                ALU.subtract).then_inc(shift_ready, 1)

            def normalise(n, qd, first):
                s = qd % 2
                wait(dve, exp_ready, 4 * n + (qd + 1))
                v.tensor_tensor(tot[:, s, :], den[:, s, :], snk_d[:, s, :], ALU.add).then_inc(tot_ready, 1)
                wait(dve, tot_ready, 4 * n + (qd + 1))
                v.reciprocal(rec[:, s, :], tot[:, s, :]).then_inc(rec_ready, 1)
                wait(dve, rec_ready, 4 * n + (qd + 1))
                lo = P if first else 0
                for i in range(4):
                    w = pr[:, s, i, lo:2 * P]
                    i_ = v.tensor_scalar(w, w, rec[:, s, i:i + 1], None, ALU.mult)
                i_.then_inc(p_ready, 1)

            def probs_lo(n, qd):
                for kb in range(2):
                    wait(dve, pt_hi, 8 * n + (2 * qd + kb + 1))
                    v.tensor_tensor(pt[:, 1, kb, :], bank[B_PT + kb][:, :], f32(pt[:, 0, kb, :]),
                                    ALU.subtract).then_inc(pt_ready, 1)

            def attention_out(n, qd):
                wait_apart(dve, pv_ready, 4 * n + (qd + 1))
                v.tensor_copy(qa[:, 2 * qd:2 * qd + 2, cols(n * P, P)],
                              bank[B_PV][:, 0:256].rearrange("p (a n) -> p a n", a=2)[:, :, ::-1]).then_inc(pv_out, 1)

            def conv(n, it, j):
                dve.wait_ge(half_ready[j], at(lambda w: w + 1, 6, 3, it))
                dve.wait_ge(free_act[j], at(lambda w: frees("A", j, w), 5, 3, it))
                v.tensor_tensor(tz[:, j, 2:T + 2], bank[j][:, :], ta[:, j, :], ALU.mult).then_inc(free_dve[j], 1)
                dve.wait_ge(free_dve[j], at(lambda w: frees("D", j, w), 6, 3, it))

                def tap(i):
                    return pcol[:, cols(n * 2 + (j + (2 + i) * KT), 1)]
                v.tensor_scalar(ty[:, j, :], tz[:, j, 2:T + 2], tap(2), None, ALU.mult).then_inc(conv1, 1)
                for i in (1, 0):
                    dve.wait_ge(conv1, n * 6 + (3 * j + 2 - i))
                    v.scalar_tensor_tensor(out=ty[:, j, :], in0=tz[:, j, i:T + i], scalar=tap(i), in1=ty[:, j, :],
                                           op0=ALU.mult, op1=ALU.add).then_inc(conv1, 1)

            def conv_gate(n, it, j):
                dve.wait_ge(half_ready[j], at(lambda w: w + 1, 7, 3, it))
                wait(dve, conv1, n * 6 + (3 * j + 3))
                v.tensor_tensor(y[:, cols(n * 2 + j, 1), :], bank[j][:, :].rearrange("p (a n) -> p a n", a=1),
                                ty[:, j:j + 1, :], ALU.mult).then_inc(free_dve[j], 1)

            def mixer_block(n, it, before):
                first = before is None
                if not first:
                    probs_lo(before, 2)
                stage_queries(n)
                lo_chunks(S_MIX + 1, 3, it)
                if not first:
                    attention_out(before, 2)
                add_bias(n, 0, first)
                if not first:
                    probs_lo(before, 3)
                lo_chunks(S_MIX + 2, 3, it)
                if not first:
                    attention_out(before, 3)
                add_bias(n, 1, first)
                normalise(n, 0, first)
                stage_values(n)
                conv(n, it, 0)
                probs_lo(n, 0)
                conv(n, it, 1)
                add_bias(n, 2, first)
                normalise(n, 1, first)
                lo_chunks(S_MIX + 3, 3, it)
                attention_out(n, 0)
                conv_gate(n, it, 0)
                probs_lo(n, 1)
                normalise(n, 2, first)
                add_bias(n, 3, first)
                conv_gate(n, it, 1)
                attention_out(n, 1)
                normalise(n, 3, first)

            dve.wait_ge(bias_in, 16)
            dve.wait_ge(zeroed, N_ZEROED)
            mixer_block(0, 0, None)
            with dve.Fori(1, TB) as n:
                mixer_block(n, Pass(n, 1, TB), n - 1)

            def split(dst, src, e, done):
                dve.wait_ge(sp_hi, done + 1)
                v.tensor_tensor(dst[:, 1, 4 * e:4 * e + 4, :], src[:, 4 * e:4 * e + 4, :],
                                f32(dst[:, 0, 4 * e:4 * e + 4, :]), ALU.subtract).then_inc(sp_ready, 1)

            def branch_group(it, first):
                i = index(it)
                if first:
                    probs_lo(3, 2)
                lo_chunks(S_OUT + 1, 4, it)
                if first:
                    split(ysplit, y, 0, 0)
                    attention_out(3, 2)
                    probs_lo(3, 3)
                    split(ysplit, y, 1, 1)
                    attention_out(3, 3)
                lo_chunks(S_OUT + 2, 4, it)
                if first:
                    split(asplit, qa, 0, 2)
                    split(asplit, qa, 1, 3)
                for j in range(2):
                    dve.wait_ge(half_ready[j], at(lambda w: w + 1, 18, 4, it))
                    dve.wait_ge(free_act[j], at(lambda w: frees("A", j, w), 17, 4, it))
                    v.tensor_tensor(tz[:, j, 0:T], bank[j][:, :], ta[:, j, :], ALU.mult).then_inc(free_dve[j], 1)
                lo_chunks(S_OUT + 3, 4, it)
                lo_chunks(S_OUT + 4, 4, it)
                for j in range(2):
                    dve.wait_ge(half_ready[j], at(lambda w: w + 1, 20, 4, it))
                    dve.wait_ge(free_act[j], at(lambda w: frees("A", j, w), 19, 4, it))
                    v.tensor_tensor(ty[:, j, :], bank[j][:, :], ta[:, j, :], ALU.mult).then_inc(free_dve[j], 1)
                    dve.wait_ge(free_dve[j], at(lambda w: frees("D", j, w), 20, 4, it))
                    v.tensor_tensor(ty[:, j, :], ty[:, j, :], tz[:, j, 0:T], ALU.add).then_inc(mix_f, 1)
                    dve.wait_ge(mix_f, i * 2 + (j + 1))
                    dve.wait_ge(mix_hi, i * 2 + (j + 1))
                    v.tensor_tensor(mix[:, 1, cols(i * 2 + j, 1), :], ty[:, j:j + 1, :],
                                    f32(mix[:, 0, cols(i * 2 + j, 1), :]), ALU.subtract).then_inc(mix_ready, 1)

            branch_group(0, True)
            with dve.Fori(1, 4) as j:
                branch_group(Pass(j, 1, 4), False)

            def norm_lo(ch):
                for f in range(4):
                    k = 4 * ch + f
                    dve.wait_ge(h2_hi, k + 1)
                    v.scalar_tensor_tensor(out=h[:, 1, k, :], in0=bank[4 + f][:, :], scalar=pcol[:, g2 + k:g2 + k + 1],
                                           in1=f32(h[:, 0, k, :]), op0=ALU.mult, op1=ALU.subtract).then_inc(h2_ready, 1)

            def add_mixers(ch):
                for b in range(TB):
                    dve.wait_ge(row_ready, 4 * ch + b + 1)
                    r = res[:, b, 512 * ch:512 * ch + 512]
                    v.tensor_tensor(r, bank[4 + b if ch == 0 else b][:, :], r, ALU.add).then_inc(row_free, 1)

            lo_chunks(S_WO + 1)
            dve.wait_ge(res_in, 32)
            lo_chunks(S_WO + 2)
            add_mixers(0)
            lo_chunks(S_WO + 3)
            norm_lo(0)
            lo_chunks(S_MLP)
            add_mixers(1)
            norm_lo(1)

            def add_mlp(i, ch, b):
                wait(dve, row_ready, i * 8 + (8 + 4 * ch + b + 1))
                r = res[:, b, 512 * ch:512 * ch + 512]
                v.scalar_tensor_tensor(out=r, in0=bank[4 + b if ch == 0 else b][:, :], scalar=rr2[:, 1, b:b + 1],
                                       in1=r, op0=ALU.mult, op1=ALU.add).then_inc(row_free, 1)

            def final_norm(b):
                dve.wait_ge(root3_done, b + 1)
                v.reciprocal(rms3[:, 2, b:b + 1], rms3[:, 1, b:b + 1]).then_inc(fin_step, 1)
                dve.wait_ge(fin_step, b + 1)
                r = res[:, b, 512:D]
                v.scalar_tensor_tensor(out=r, in0=r, scalar=rms3[:, 2, b:b + 1], in1=gfin[:, 512:D],
                                       op0=ALU.mult, op1=ALU.mult).then_inc(out_right, 1)

            def mlp_quarter(it, first=False, last=False):
                i = index(it)
                for u in range(4):
                    lo_chunks(S_MLP + u + 1, 8, it)
                    for j in range(2):
                        dve.wait_ge(free_act[j], at(lambda w: frees("A", j, w), 33 + u, 4, it))
                        v.tensor_tensor(ty[:, j, :], ta[:, j, :], ta[:, j, :], ALU.mult).then_inc(sqr, 1)
                        wait(dve, sqr, i * 8 + (2 * u + j + 1))
                        wait(dve, hid_hi, i * 8 + (2 * u + j + 1))
                        v.tensor_tensor(hid[:, 1, 2 * u + j, :], ty[:, j, :], f32(hid[:, 0, 2 * u + j, :]),
                                        ALU.subtract).then_inc(hid_ready, 1)
                    if first and u == 0:
                        dve.wait_ge(ss2_ready, TB)
                        v.tensor_scalar(rr2[:, 0, :], ss2[:, :], 1.0 / D, EPS, ALU.mult, ALU.add).then_inc(rr2_step, 1)
                        dve.wait_ge(rr2_step, 1)
                        v.reciprocal(rr2[:, 1, :], rr2[:, 0, :]).then_inc(rr2_step, 1)
                        dve.wait_ge(rr2_step, 2)
                for u in range(4):
                    if not (last and u == 3):
                        lo_chunks(S_MLP + u + 5, 8, it)
                    if last and u == 2:
                        for b in range(TB):
                            dve.wait_ge(ss3_ready, b + 1)
                            r = res[:, b, 0:512]
                            v.tensor_tensor(r, r, gfin[:, 0:512], ALU.mult).then_inc(gained, 1)
                    if u % 2 == 1:
                        for b in range(TB):
                            add_mlp(i, u // 2, b)
                            if last and u == 3:
                                final_norm(b)

            mlp_quarter(0, first=True)
            with dve.Fori(1, 3) as i:
                mlp_quarter(Pass(i, 1, 3))
            mlp_quarter(3, last=True)


INPUTS = ["x", "attn_norm_g", "w_in", "conv_w", "w_conv_out", "attn_sinks", "rel_bias", "w_attn_out", "w_o",
          "mlp_norm_g", "w_up", "w_down", "final_norm_g"]


def kernel(**inputs):
    import concourse.bacc as bacc
    from concourse.bass_utils import run_bass_kernel_spmd

    nc = bacc.Bacc("TRN2", target_bir_lowering=False, num_devices=1)
    arrays, args = {}, []
    for name in INPUTS:
        v = np.ascontiguousarray(inputs[name])
        arrays[f"in_{name}"] = v
        t = nc.dram_tensor(f"in_{name}", v.shape, mybir.dt.from_np(v.dtype), kind="ExternalInput").ap()
        drop = name in ("x", "w_in", "w_conv_out", "w_attn_out", "w_o", "w_up", "w_down")
        args.append(t.rearrange("a b c -> (a b) c") if drop else t)
    result = nc.dram_tensor("out_0", (1, T, D), F32, kind="ExternalOutput").ap()
    build(nc, *args, result.rearrange("a b c -> (a b) c"))
    r = run_bass_kernel_spmd(nc, [arrays], core_ids=[0])
    return r.results[0]["out_0"]
```

```python
from contextlib import ExitStack

import numpy as np

import concourse.bass as bass
from concourse import mybir

F32 = mybir.dt.float32
F32R = mybir.dt.float32r
ALU = mybir.AluOpType
ACT = mybir.ActivationFunctionType

P = 128
D = 1024
T = 512
KT = D // P
TB = T // P
HEADS, KV, HD = 16, 2, 64
QUADS = 4
WINDOW, BUCKETS, MAX_DIST = 128, 32, 128
FF = 4 * D
EPS, NEG = 1e-6, -1e30
SCALE = HD ** -0.5

COL_B, COL_C, COL_X, COL_Q = 0, D, 2 * D, 3 * D
COL_KV = 4 * D
COL_GC = COL_KV + 2 * KV * HD
COL_GA = COL_GC + D

SC = 256
S_KV, S_Q = 0, 1
S_MIX = S_Q + 4
S_OUT = S_MIX + 3 * 4
S_WO = S_OUT + 4 * 4
S_MLP = S_WO + 4
STRIPS = S_MLP + 8 * 4


def t5_bucket(dist):
    n = np.maximum(dist, 0)
    exact = BUCKETS // 2
    ratio = np.log(np.maximum(n, exact).astype(np.float32) / exact) / np.log(MAX_DIST / exact)
    large = np.minimum(exact + (ratio * (BUCKETS - exact)).astype(np.int32), BUCKETS - 1)
    return np.where(n < exact, n, large)


def weight_slot(s):
    if s < S_MIX:
        return 0 if s == S_KV else (1, 2)[(s - S_Q) % 2]
    if s < S_OUT:
        return (1, 0, 2)[(s - S_MIX) % 3]
    return (1, 0, 2, 0)[(s - S_OUT) % 4]


def raw_slot(c):
    if c < 2 * S_Q:
        return 2 + c
    if c < 2 * S_MIX:
        return (c - 2 * S_Q) % 4
    if c < 2 * S_OUT:
        return (c - 2 * S_MIX) % 3
    return (0, 1, 3, 2)[(c - 2 * S_OUT) % 4]


def raw_uses(c):
    return sum(raw_slot(x) == raw_slot(c) for x in range(c + 1))


def raw_back(c):
    return next((d for d in range(1, c + 1) if raw_slot(c - d) == raw_slot(c)), None)


KINDS = (["kv"] + ["q"] * 4 + ["c", "x", "b"] * 4 + ["gc", "co", "ga", "ao"] * 4 + ["up"] * 16)
FREES = {"kv": "AD", "q": "AD", "c": "AA", "x": "DD", "b": "DD", "gc": "AA", "co": "DD", "ga": "AA",
         "ao": "DD", "up": "AA"}


def row_matrix(s):
    if S_WO <= s < S_MLP:
        return 0
    return (s - S_MLP) // 8 + 1 if s >= S_MLP and (s - S_MLP) % 8 >= 4 else None


def transposed_before(s):
    return sum(row_matrix(x) is None for x in range(s))


def frees(engine, half, t):
    return sum(FREES[KINDS[x]][half] == engine for x in range(t + 1))


class Pass:

    def __init__(self, reg, first, end):
        self.reg, self.first, self.end = reg, first, end


def at(f, x, step, it):
    if isinstance(it, int):
        return f(x + step * it)
    v = [f(x + step * i) for i in range(it.first, it.end)]
    slope = v[1] - v[0]
    assert all(b - a == slope for a, b in zip(v, v[1:]))
    return it.reg * slope + (v[0] - slope * it.first)


def keys_of(n):
    return ((1,), P) if isinstance(n, int) and n == 0 else ((0, 1), 0)


def index(it):
    return it if isinstance(it, int) else it.reg


def first_of(it):
    return it if isinstance(it, int) else it.first


def build(nc, x, attn_norm_g, w_in, conv_w, w_conv_out, attn_sinks, rel_bias, w_attn_out, w_o,
          mlp_norm_g, w_up, w_down, final_norm_g, out):
    ctx = ExitStack()
    with ctx:
        base = -(-nc.sbuf_base // 64) * 64
        top = [base]

        def place(name, shape, dt=F32, offset=None):
            size = 4 * int(np.prod(shape[1:]))
            if offset is None:
                offset = top[0]
                top[0] = -(-(offset + size) // 64) * 64
            return nc.alloc_sbuf_tensor_at(name, shape, dt, offset=offset)

        raw = [place(f"raw{i}", [P, 1024]) for i in range(4)]
        wgt = [place(f"wgt{i}", [P, 2, 2048], F32R) for i in range(3)]
        h = place("h", [P, 2, KT, T], F32R)
        qa_at = top[0]
        qa = place("qa", [P, KT, T])
        y = place("y", [P, KT, T])
        mix = place("mix", [P, 2, KT, T], F32R, offset=qa_at)
        hid = place("hid", [P, 2, KT, T], F32R, offset=qa_at)
        one_at = top[0]
        bias = place("bias", [P, HEADS, 2 * P])
        qs = place("qs", [P, KT, 2, P], F32R)
        khi = place("khi", [P, KV, T], F32R)
        vnat = place("vnat", [P, TB, KV * HD])
        xn = place("xn", [P, TB, D], offset=one_at)
        ysplit = place("ysplit", [P, 2, KT, T], F32R, offset=one_at)
        top[0] = max(top[0], one_at + 4 * 2 * KT * T)
        two_at = top[0]
        klo = place("klo", [P, KV, T], F32R)
        pr = place("pr", [P, 2, 4, 2 * P])
        pt = place("pt", [P, 2, 2, 4 * P], F32R)
        vs = place("vs", [P, 2, KV, 2, HD], F32R)
        pv_low = place("pv_low", [HD, T])
        asplit = place("asplit", [P, 2, KT, T], F32R, offset=two_at)
        res = place("res", [P, TB, D], offset=two_at)
        gfin = place("gfin", [P, D], offset=two_at + 4 * TB * D)
        top[0] = max(top[0], two_at + 4 * 2 * KT * T)
        ta = place("ta", [P, 2, T])
        tz = place("tz", [P, 2, T + 2])
        ty = place("ty", [P, 2, T])
        ident = place("ident", [P, P])
        prow = place("prow", [5 * KT, P])
        pcol = place("pcol", [P, 5 * KT])
        rbt = place("rbt", [HEADS, BUCKETS])
        ext = place("ext", [HEADS, 3 * P])
        sink = place("sink", [P, HEADS])
        eps = place("eps", [P, 1])
        ssq = place("ssq", [P, TB])
        rms = place("rms", [P, 2, TB])
        ss2 = place("ss2", [P, TB])
        rr2 = place("rr2", [P, 2, TB])
        ss3 = place("ss3", [P, 2, TB])
        rms3 = place("rms3", [P, 3, TB])
        top_m = place("top_m", [P, 2, 4])
        neg_m = place("neg_m", [P, 2, 4])
        snk_d = place("snk_d", [P, 2, 4])
        den = place("den", [P, 2, 4])
        tot = place("tot", [P, 2, 4])
        rec = place("rec", [P, 2, 4])
        g1, g2 = 0, KT
        bias_rows = nc.dram_tensor("bias_rows", (HEADS, 3 * P), F32)

        bank = [ctx.enter_context(nc.psum_tensor(f"bank{i}", [P, T], F32)) for i in range(8)]
        B_SC, B_PT, B_PV, B_VT = 2, 4, 6, 7

        def sem(name):
            return ctx.enter_context(nc.semaphore(name))

        x_in = [sem(f"x_in{b}") for b in range(TB)]
        raw_in = [sem(f"raw_in{i}") for i in range(4)]
        rows_in, table_in, bias_out, bias_in, res_in, out_done = (
            sem(n) for n in ("rows_in", "table_in", "bias_out", "bias_in", "res_in", "out_done"))
        hi_ready, lo_ready, row_part = sem("hi_ready"), sem("lo_ready"), sem("row_part")
        half_ready = [sem(f"half_ready{j}") for j in range(2)]
        free_act = [sem(f"free_act{j}") for j in range(2)]
        free_dve = [sem(f"free_dve{j}") for j in range(2)]
        ident_step, zeroed, ext_step = sem("ident_step"), sem("zeroed"), sem("ext_step")
        par_t, par_ready = sem("par_t"), sem("par_ready")
        sq_done, rms_step, xn_ready, xt_ready = sem("sq_done"), sem("rms_step"), sem("xn_ready"), sem("xt_ready")
        h_hi, h_ready = sem("h_hi"), sem("h_ready")
        k_hi, vt_done, v_ready, conv1 = sem("k_hi"), sem("vt_done"), sem("v_ready"), sem("conv1")
        qs_hi, qs_ready, vs_hi, vs_ready = sem("qs_hi"), sem("qs_ready"), sem("vs_hi"), sem("vs_ready")
        qk_ready, logits, shift_ready, exp_ready = (sem(n) for n in
                                                    ("qk_ready", "logits", "shift_ready", "exp_ready"))
        tot_ready, rec_ready, p_ready = sem("tot_ready"), sem("rec_ready"), sem("p_ready")
        t_ready, pt_hi, pt_ready, pv_ready, pv_out = (sem(n) for n in
                                                      ("t_ready", "pt_hi", "pt_ready", "pv_ready", "pv_out"))
        low_out = sem("low_out")
        sp_hi, sp_ready = sem("sp_hi"), sem("sp_ready")
        mix_f, mix_hi, mix_ready = sem("mix_f"), sem("mix_hi"), sem("mix_ready")
        row_ready, row_free = sem("row_ready"), sem("row_free")
        rt_ready, h2_hi, h2_ready = sem("rt_ready"), sem("h2_hi"), sem("h2_ready")
        ss2_ready, rr2_step = sem("ss2_ready"), sem("rr2_step")
        sqr, hid_hi, hid_ready = sem("sqr"), sem("hid_hi"), sem("hid_ready")
        passed = sem("passed")
        root_done, root3_part, root3_done = sem("root_done"), sem("root3_part"), sem("root3_done")
        ss3_ready, gained, fin_step = sem("ss3_ready"), sem("gained"), sem("fin_step")
        out_left, out_right = sem("out_left"), sem("out_right")

        def wait(eng, s, value):
            if not isinstance(value, int) or value > 0:
                eng.wait_ge(s, value)

        def wait_apart(eng, s, value):
            wait(eng, s, value)
            if not isinstance(value, int):
                eng.sem_inc(passed, 1)

        def f32(ap):
            return ap.bitcast(F32)

        def cols(start, size):
            return bass.ds(start, size)

        block = ctx.enter_context(nc.Block())

        @block.sync
        def _(sp):
            def load_chunk(c, step, it, src):
                its = [it] if isinstance(it, int) else range(it.first, it.end)
                backs = [raw_back(c + step * i) for i in its]
                n = raw_slot(c + step * first_of(it))
                assert all(raw_slot(c + step * i) == n for i in its)
                if backs[0] is not None:
                    wait_apart(sp, lo_ready, at(lambda v: v - min(backs) + 1, c, step, it))
                dst = raw[n][:, :].rearrange("p (k n) -> p k n", k=src.shape[1])
                sp.dma_start(dst, src).then_inc(raw_in[n], 16)

            def load_t(s, step, it, w, col):
                v = w.rearrange("(k p) n -> p k n", p=P)
                for a in range(2):
                    load_chunk(2 * s + a, 2 * step, it, v[:, 4 * a:4 * a + 4, cols(col, SC)])

            def load_row(s, step, it, w, row_tile, col):
                v = w.rearrange("(k p) n -> p k n", p=P)
                for a in range(2):
                    load_chunk(2 * s + a, 2 * step, it, v[:, cols(row_tile + 2 * a, 2), col:col + 512])

            for b in range(TB):
                sp.dma_start(xn[:, b, :], x[b * P:(b + 1) * P, :]).then_inc(x_in[b], 16)
            load_t(S_KV, 0, 0, w_in, COL_KV)
            load_t(S_Q, 0, 0, w_in, COL_Q)
            sp.wait_ge(ext_step, 1 + BUCKETS)
            sp.dma_start(bias_rows[:, :], ext[:, :]).then_inc(bias_out, 16)
            sp.wait_ge(bias_out, 16)
            sp.wait_ge(xt_ready, TB)
            band = bass.AP(bias_rows, 0, [[1, P], [3 * P, HEADS], [1, 2 * P]])
            sp.dma_start(bias[:, :, :], band).then_inc(bias_in, 16)
            for i in range(1, 4):
                load_t(S_Q + i, 0, 0, w_in, COL_Q + SC * i)
            with sp.Fori(0, 4) as n:
                it = Pass(n, 0, 4)
                load_t(S_MIX, 3, it, w_in, n * SC + COL_C)
                load_t(S_MIX + 1, 3, it, w_in, n * SC + COL_X)
                load_t(S_MIX + 2, 3, it, w_in, n * SC + COL_B)
            with sp.Fori(0, 4) as n:
                it = Pass(n, 0, 4)
                load_t(S_OUT, 4, it, w_in, n * SC + COL_GC)
                load_t(S_OUT + 1, 4, it, w_conv_out, n * SC)
                load_t(S_OUT + 2, 4, it, w_in, n * SC + COL_GA)
                load_t(S_OUT + 3, 4, it, w_attn_out, n * SC)
            for i in range(4):
                load_row(S_WO + i, 0, 0, w_o, 4 * (i % 2), 512 * (i // 2))
            with sp.Fori(0, 4) as i:
                it = Pass(i, 0, 4)
                for u in range(4):
                    load_t(S_MLP + u, 8, it, w_up, i * D + SC * u)
                for u in range(4):
                    load_row(S_MLP + 4 + u, 8, it, w_down, i * KT + 4 * (u % 2), 512 * (u // 2))
            for b in range(TB):
                for ch in range(2):
                    sp.wait_ge((out_left, out_right)[ch], b + 1)
                    sp.dma_start(out[b * P:(b + 1) * P, 512 * ch:512 * ch + 512],
                                 res[:, b, 512 * ch:512 * ch + 512]).then_inc(out_done, 16)
            sp.wait_ge(out_done, 16 * 2 * TB)

        @block.gpsimd
        def _(pool):
            g = nc.gpsimd
            g.memset(ident[:, :], 0.0).then_inc(ident_step, 1)
            g.memset(eps[:, :], EPS).then_inc(ident_step, 1)
            pool.wait_ge(ident_step, 2)
            g.affine_select(out=ident[:, :], in_=ident[:, :], compare_op=ALU.not_equal, fill=1.0, base=0,
                            pattern=[[-1, P]], channel_multiplier=1).then_inc(ident_step, 1)
            with nc.allow_non_contiguous_dma("a table of 32 x 16"):
                pool.dma_start(rbt[:, :], rel_bias.rearrange("b h -> h b")).then_inc(table_in, 16)
            pool.dma_start(sink[:, :], bass.AP(attn_sinks.tensor, 0, [[0, P], [1, HEADS]])).then_inc(table_in, 16)
            g.memset(ext[:, :], NEG).then_inc(ext_step, 1)
            pool.wait_ge(table_in, 16 * 2)
            pool.wait_ge(ext_step, 1)
            bucket = t5_bucket(np.arange(WINDOW))
            for b in range(BUCKETS):
                dist = np.flatnonzero(bucket == b)
                m0, n = 2 * P - 1 - int(dist[-1]), len(dist)
                g.tensor_copy(ext[:, m0:m0 + n], rbt[:, b:b + 1].to_broadcast([HEADS, n])).then_inc(ext_step, 1)
            for t in (pr[:, :, :, 0:P], f32(vs[:, 0, :, :, :]), tz[:, :, 0:2]):
                g.memset(t, 0.0).then_inc(zeroed, 1)
        N_ZEROED = 3

        @block.tensor
        def _(pe):
            mm = nc.tensor.matmul

            def transposed_strip(s, step, it, t, tstep, rhs, hooks={}, k_wait=None,
                                 bank_wait=None, by_chunk=False, swapped=False):
                first = first_of(it)
                w = wgt[weight_slot(s + step * first)][:, :, :].rearrange("p c (k n) -> p c k n", k=KT)
                quarters = [(j, e) for j in range(2) for e in range(2)]
                if by_chunk:
                    quarters = [(j, e) for e, j in quarters]
                for q, (j, e) in enumerate(quarters):
                    if e == 0 and t + tstep * first > 0:
                        who = FREES[KINDS[t - 1 + tstep * first]][j]
                        wait(pe, (free_act if who == "A" else free_dve)[j],
                             at(lambda v: frees(who, j, v), t - 1, tstep, it))
                    if e == 0 and bank_wait:
                        bank_wait(j)
                    if j == 0:
                        wait(pe, lo_ready, at(lambda v: 2 * v + e + 1, s, step, it))
                    for k in range(4 * e, 4 * e + 4):
                        if j == 0 and k_wait:
                            k_wait(k)
                        half = cols((1 - j if swapped else j) * P, P)
                        wh, wl = w[:, 0, k, half], w[:, 1, k, half]
                        mm(bank[j][:, :], wh, rhs[:, 0, k, :], start=(k == 0), stop=False)
                        mm(bank[j][:, :], wh, rhs[:, 1, k, :], start=False, stop=False)
                        last = mm(bank[j][:, :], wl, rhs[:, 0, k, :], start=False, stop=(k == KT - 1))
                    if e == 1:
                        last.then_inc(half_ready[j], 1)
                    for f in hooks.get(q, ()):
                        f()

            def row_strip(s, step, it, m, ch, kh, lhs, k_wait=None, hooks={}):
                w = wgt[weight_slot(s + step * first_of(it))][:, :, :].rearrange("p c (k n) -> p c k n", k=4)
                for b in range(TB):
                    acc = bank[4 + b if ch == 0 else b]
                    if kh == 0 and (not isinstance(m, int) or m > 0):
                        wait(pe, row_free, 8 * (m - 1) + (4 * ch + b + 1))
                    for kk in range(4):
                        k = 4 * kh + kk
                        if b == 0 and kk % 2 == 0:
                            wait(pe, lo_ready, at(lambda v: 2 * v + kk // 2 + 1, s, step, it))
                        if b == 0 and k_wait:
                            k_wait(k)
                        lh = lhs[:, 0, k, b * P:(b + 1) * P]
                        ll = lhs[:, 1, k, b * P:(b + 1) * P]
                        mm(acc[:, :], lh, w[:, 0, kk, :], start=(k == 0), stop=False)
                        mm(acc[:, :], ll, w[:, 0, kk, :], start=False, stop=False)
                        last = mm(acc[:, :], lh, w[:, 1, kk, :], start=False, stop=(k == KT - 1))
                        if k == KT - 1:
                            last.then_inc(row_ready, 1)
                        elif kk == 3 and b == TB - 1:
                            last.then_inc(row_part, 1)
                    for f in hooks.get(b, ()):
                        f()

            def scores(n, qd):
                if qd == 0:
                    pe.wait_ge(free_dve[1], 1)
                    wait(pe, qs_ready, 2 * n + 2)
                wait(pe, logits, 4 * n + qd)
                kbs, lo = keys_of(n)
                keys = cols((n + kbs[0] - 1) * P, len(kbs) * P)
                for i in range(4):
                    head = 4 * qd + i
                    acc = bank[B_SC + i // 2][:, 256 * (i % 2) + lo:256 * (i % 2) + 256]
                    q = qs[:, head // 2, head % 2, :]
                    kg = head // (HEADS // KV)
                    mm(acc, q, khi[:, kg, keys], start=True, stop=False)
                    last = mm(acc, q, klo[:, kg, keys], start=False, stop=True)
                last.then_inc(qk_ready, 1)

            def transpose_probs(n, qd):
                wait(pe, p_ready, 4 * n + (qd + 1))
                wait(pe, pt_ready, 8 * n + 2 * qd)
                kbs, _ = keys_of(n)
                for kb in kbs:
                    for i in range(4):
                        c = 2 * (i % 2) + i // 2
                        last = nc.tensor.transpose(bank[B_PT + kb][:, c * P:(c + 1) * P],
                                                   pr[:, qd % 2, i, kb * P:(kb + 1) * P], ident[:, :])
                    last.then_inc(t_ready, 2 // len(kbs))

            def values(n, qd):
                wait(pe, pt_ready, 8 * n + (2 * qd + 2))
                if qd == 0:
                    wait(pe, vs_ready, n + 1)
                wait(pe, pv_out, 4 * n + qd)
                kg = qd // 2
                steps = [(kb, part) for kb in keys_of(n)[0] for part in range(2)]
                for e, (kb, part) in enumerate(steps):
                    last = mm(bank[B_PV][:, :], vs[:, kb, kg, :, :].rearrange("p a d -> p (a d)"), pt[:, part, kb, :],
                              start=(e == 0), stop=(e == len(steps) - 1))
                last.then_inc(pv_ready, 1)

            def x_transpose(b, k):
                return nc.tensor.transpose(bank[k][:, b * P:(b + 1) * P], xn[:, b, k * P:(k + 1) * P], ident[:, :])

            pe.wait_ge(ident_step, 3)
            for b in range(TB):
                pe.wait_ge(xn_ready, b + 1)
                for k in range(KT - 1):
                    x_transpose(b, k)
                if b == 0:
                    pe.wait_ge(rows_in, 16 * 3)
                    nc.tensor.transpose(bank[KT - 1][:, 0:5 * KT], prow[:, :],
                                        ident[0:5 * KT, 0:5 * KT]).then_inc(par_t, 1)
                    continue
                if b == 1:
                    pe.wait_ge(par_ready, 1)
                    x_transpose(0, KT - 1).then_inc(xt_ready, 1)
                x_transpose(b, KT - 1).then_inc(xt_ready, 1)

            def first_tile(k):
                pe.wait_ge(h_ready, k + 1)

            transposed_strip(S_KV, 0, 0, 0, 0, h, k_wait=first_tile, by_chunk=True, swapped=True)

            def value_transposes():
                pe.wait_ge(free_act[0], 1)
                for b in range(TB):
                    last = nc.tensor.transpose(bank[B_VT][:, b * P:(b + 1) * P], ty[:, 1, b * P:(b + 1) * P],
                                               ident[:, :])
                last.then_inc(vt_done, 1)

            with pe.Fori(0, 2) as i:
                it = Pass(i, 0, 2)
                transposed_strip(S_Q, 2, it, 1, 2, h)
                transposed_strip(S_Q + 1, 2, it, 2, 2, h)
            value_transposes()

            def mixer_block(n, it, before):
                def on(f, m, qd):
                    return lambda: f(m, qd)
                prev = before is not None
                transposed_strip(S_MIX, 3, it, 5, 3, h, hooks={
                    1: [on(values, before, 2)] if prev else [],
                    2: [on(scores, n, 0)] + ([on(transpose_probs, before, 3)] if prev else [])})
                transposed_strip(S_MIX + 1, 3, it, 6, 3, h, hooks={
                    0: ([on(values, before, 3)] if prev else []) + [on(scores, n, 1)],
                    2: [on(transpose_probs, n, 0)],
                    3: [on(scores, n, 2)]})
                transposed_strip(S_MIX + 2, 3, it, 7, 3, h, hooks={
                    0: [on(values, n, 0)],
                    1: [on(transpose_probs, n, 1)],
                    2: [on(scores, n, 3)],
                    3: [on(values, n, 1), on(transpose_probs, n, 2)]})

            mixer_block(0, 0, None)
            with pe.Fori(1, TB) as n:
                mixer_block(n, Pass(n, 1, TB), n - 1)

            def branch_group(it, hooks={}):
                transposed_strip(S_OUT, 4, it, 17, 4, h, hooks=hooks)
                transposed_strip(S_OUT + 1, 4, it, 18, 4, ysplit,
                                 k_wait=lambda k: pe.wait_ge(sp_ready, k // 4 + 1) if k % 4 == 0 else None)
                transposed_strip(S_OUT + 2, 4, it, 19, 4, h)
                transposed_strip(S_OUT + 3, 4, it, 20, 4, asplit,
                                 k_wait=lambda k: pe.wait_ge(sp_ready, k // 4 + 3) if k % 4 == 0 else None)

            branch_group(0, {1: [lambda: values(3, 2), lambda: transpose_probs(3, 3)], 3: [lambda: values(3, 3)]})
            with pe.Fori(1, 4) as j:
                branch_group(Pass(j, 1, 4))

            def residual_transposes(b, ch):
                pe.wait_ge(row_free, 4 * ch + b + 1)
                if ch == 0 and b == 0:
                    pe.wait_ge(row_free, TB)
                if ch == 1 and b == 0:
                    pe.wait_ge(h2_ready, 4)
                for f in range(4):
                    last = nc.tensor.transpose(bank[4 + f][:, b * P:(b + 1) * P],
                                               res[:, b, 512 * ch + f * P:512 * ch + (f + 1) * P], ident[:, :])
                last.then_inc(rt_ready, 1)

            def rt(b, ch):
                return lambda: residual_transposes(b, ch)

            row_strip(S_WO, 0, 0, 0, 0, 0, mix, k_wait=lambda k: pe.wait_ge(mix_ready, k + 1))
            row_strip(S_WO + 1, 0, 0, 0, 0, 1, mix, k_wait=lambda k: pe.wait_ge(mix_ready, k + 1))
            row_strip(S_WO + 2, 0, 0, 0, 1, 0, mix, hooks={1: [rt(0, 0), rt(1, 0)], 2: [rt(2, 0), rt(3, 0)]})
            row_strip(S_WO + 3, 0, 0, 0, 1, 1, mix, hooks={1: [rt(0, 1)], 2: [rt(1, 1)], 3: [rt(2, 1)]})

            def mlp_quarter(it, hooks={}):
                for u in range(4):
                    transposed_strip(S_MLP + u, 8, it, 33 + u, 4, h, hooks=hooks if u == 0 else {},
                                     by_chunk=isinstance(it, int) and u == 0,
                                     k_wait=lambda k: pe.wait_ge(h2_ready, k + 1) if u == 0 else None,
                                     bank_wait=lambda j: pe.wait_ge(row_free, index(it) * 8 + (5 + j))
                                     if u == 0 else None)
                for u in range(4):
                    row_strip(S_MLP + 4 + u, 8, it, index(it) + 1, u // 2, u % 2, hid,
                              k_wait=lambda k: pe.wait_ge(hid_ready, index(it) * 8 + (k + 1)) if u < 2 else None)

            mlp_quarter(0, {0: [rt(3, 1)]})
            with pe.Fori(1, 4) as i:
                mlp_quarter(Pass(i, 1, 4))

        @block.scalar
        def _(act):
            a = nc.scalar.activation

            def slot_free(s, step, it):
                s1 = s + step * first_of(it)
                if s1 < 0:
                    return
                m = row_matrix(s1)
                if m is None:
                    wait(act, half_ready[1], at(lambda v: transposed_before(v) + 1, s, step, it))
                elif (s1 - S_WO) % 2 == 0:
                    wait(act, row_part, at(lambda v: 2 * row_matrix(v) + (v - S_WO) % 4 // 2 + 1, s, step, it))
                else:
                    wait(act, row_ready, at(lambda v: 8 * row_matrix(v) + 4 * ((v - S_WO) % 4 // 2) + 4, s, step, it))

            def hi_chunks(s, step=0, it=0, chunks=(0, 1)):
                s1 = s + step * first_of(it)
                for e in chunks:
                    c, c1 = 2 * s + e, 2 * s1 + e
                    wait(act, raw_in[raw_slot(c1)], at(lambda v: 16 * raw_uses(v), c, 2 * step, it))
                    if e == 0:
                        slot_free(s - 2, step, it)
                    a(wgt[weight_slot(s1)][:, 0, 1024 * e:1024 * e + 1024], raw[raw_slot(c1)][:, :],
                      ACT.Copy).then_inc(hi_ready, 1)

            act.dma_start(prow[0:KT, :], attn_norm_g.rearrange("a (k p) -> (a k) p", p=P)).then_inc(rows_in, 16)
            act.dma_start(prow[KT:2 * KT, :], mlp_norm_g.rearrange("a (k p) -> (a k) p", p=P)).then_inc(rows_in, 16)
            act.dma_start(prow[2 * KT:5 * KT, :], conv_w.rearrange("a t (k p) -> (a t k) p", p=P)).then_inc(rows_in, 16)
            scratch = tz[:, :, :].rearrange("p a n -> p (a n)")[:, 0:D]
            act.wait_ge(ident_step, 2)
            a(rms[:, 0, 0:1], eps[:, :], ACT.Sqrt)
            for b in range(TB):
                act.wait_ge(x_in[b], 16)
                a(ta[:, :, :].rearrange("p a n -> p (a n)"), xn[:, b, :], ACT.Square,
                  accum_out=ssq[:, b:b + 1]).then_inc(sq_done, 1)
                act.wait_ge(sq_done, b + 1)
                a(rms[:, 0, b:b + 1], ssq[:, b:b + 1], ACT.Sqrt, bias=eps[:, :], scale=1.0 / D).then_inc(root_done, 1)
            hi_chunks(S_KV, chunks=(0,))
            act.wait_ge(par_ready, 1)
            act.wait_ge(xt_ready, TB)
            for k in range(KT):
                if k == KT // 2:
                    hi_chunks(S_KV, chunks=(1,))
                a(h[:, 0, k, :], bank[k][:, :], ACT.Copy, scale=pcol[:, g1 + k:g1 + k + 1]).then_inc(h_hi, 1)
            hi_chunks(S_Q)
            act.wait_ge(half_ready[0], 1)
            a(ty[:, 1, :], bank[0][:, :], ACT.Copy).then_inc(free_act[0], 1)
            act.wait_ge(half_ready[1], 1)
            for kg in range(KV):
                for up in range(2):
                    a(khi[HD * up:HD * up + HD, kg, :], bank[1][HD * kg:HD * kg + HD, :], ACT.Copy,
                      scale=SCALE).then_inc(k_hi, 1)
            with act.Fori(0, 2) as i:
                for e in range(2):
                    hi_chunks(S_Q + 1 + e, 2, Pass(i, 0, 2))
                    act.wait_ge(half_ready[0], i * 2 + (2 + e))
                    a(qa[:, cols(i * 4 + 2 * e, 1), :], bank[0][:, :].rearrange("p (a n) -> p a n", a=1),
                      ACT.Copy).then_inc(free_act[0], 1)

            def stage_queries(n):
                wait(act, qk_ready, 4 * n)
                act.wait_ge(free_dve[1], frees("D", 1, S_MIX - 1))
                act.wait_ge(free_act[0], frees("A", 0, S_MIX - 1))
                for par in range(2):
                    half = slice(HD * par, HD * par + HD)
                    a(qs[half, :, par, ::-1], qa[half, :, cols(n * P, P)], ACT.Copy).then_inc(qs_hi, 1)

            def stage_values(n):
                if isinstance(n, int):
                    act.wait_ge(v_ready, 1)
                wait(act, pv_ready, 4 * n)
                kbs, _ = keys_of(n)
                blocks = cols(n + kbs[0] - 1, len(kbs))
                a(vs[:, kbs[0]:2, :, 0, :], vnat[:, blocks, :].rearrange("p b (g d) -> p b g d", g=KV),
                  ACT.Copy).then_inc(vs_hi, 1)

            def exponentials(n, qd):
                wait(act, shift_ready, 4 * n + (qd + 1))
                _, lo = keys_of(n)
                for i in range(4):
                    v = pr[:, qd % 2, i, lo:2 * P]
                    a(v, v, ACT.Exp, bias=neg_m[:, qd % 2, i:i + 1], accum_out=den[:, qd % 2, i:i + 1])
                a(snk_d[:, qd % 2, :], snk_d[:, qd % 2, :], ACT.Exp).then_inc(exp_ready, 1)

            def probs_hi(n, qd):
                wait(act, pv_ready, 4 * n + qd)
                kbs, _ = keys_of(n)
                for kb in kbs:
                    wait(act, t_ready, 8 * n + (2 * qd + kb + 1))
                    a(pt[:, 0, kb, :], bank[B_PT + kb][:, :], ACT.Copy).then_inc(pt_hi, 2 // len(kbs))

            def lo_share(n, qd):
                wait(act, pv_ready, 4 * n + (qd + 1))
                a(pv_low[:, :], bank[B_PV][HD:2 * HD, :], ACT.Copy).then_inc(low_out, 1)

            def mixer_block(n, it, before):
                if before is not None:
                    probs_hi(before, 2)
                stage_queries(n)
                hi_chunks(S_MIX + 1, 3, it)
                if before is not None:
                    lo_share(before, 2)
                for j in range(2):
                    act.wait_ge(half_ready[j], at(lambda v: v + 1, 5, 3, it))
                    a(ta[:, j, :], bank[j][:, :], ACT.Copy).then_inc(free_act[j], 1)
                    if j == 0 and before is not None:
                        probs_hi(before, 3)
                hi_chunks(S_MIX + 2, 3, it)
                if before is not None:
                    lo_share(before, 3)
                exponentials(n, 0)
                stage_values(n)
                exponentials(n, 1)
                probs_hi(n, 0)
                hi_chunks(S_MIX + 3, 3, it)
                exponentials(n, 2)
                lo_share(n, 0)
                probs_hi(n, 1)
                lo_share(n, 1)
                exponentials(n, 3)

            mixer_block(0, 0, None)
            with act.Fori(1, TB) as n:
                mixer_block(n, Pass(n, 1, TB), n - 1)

            def split(dst, src, e):
                a(dst[:, 0, 4 * e:4 * e + 4, :], src[:, 4 * e:4 * e + 4, :], ACT.Copy).then_inc(sp_hi, 1)

            def gate(j, t, it):
                used = at(lambda v: frees("D", j, v - 1), t, 4, it)
                act.wait_ge(half_ready[j], at(lambda v: v + 1, t, 4, it))
                act.wait_ge(free_dve[j], used)
                a(ta[:, j, :], bank[j][:, :], ACT.Sigmoid).then_inc(free_act[j], 1)

            def branch_group(it, first):
                if first:
                    probs_hi(3, 2)
                hi_chunks(S_OUT + 1, 4, it)
                if first:
                    act.wait_ge(free_dve[1], frees("D", 1, 16))
                    act.wait_ge(vs_ready, TB)
                    act.wait_ge(logits, QUADS * TB)
                    split(ysplit, y, 0)
                gate(0, 17, it)
                if first:
                    lo_share(3, 2)
                    probs_hi(3, 3)
                    split(ysplit, y, 1)
                gate(1, 17, it)
                if first:
                    lo_share(3, 3)
                hi_chunks(S_OUT + 2, 4, it)
                if first:
                    act.wait_ge(pv_out, QUADS * TB)
                    split(asplit, qa, 0)
                    split(asplit, qa, 1)
                hi_chunks(S_OUT + 3, 4, it)
                gate(0, 19, it)
                gate(1, 19, it)
                hi_chunks(S_OUT + 4, 4, it)
                for j in range(2):
                    act.wait_ge(mix_f, index(it) * 2 + (j + 1))
                    a(mix[:, 0, cols(index(it) * 2 + j, 1), :], ty[:, j:j + 1, :], ACT.Copy).then_inc(mix_hi, 1)

            branch_group(0, True)
            with act.Fori(1, 4) as j:
                branch_group(Pass(j, 1, 4), False)

            a(rms3[:, 1, 0:1], eps[:, :], ACT.Sqrt)

            def norm_hi(ch):
                act.wait_ge(rt_ready, TB * (ch + 1))
                for f in range(4):
                    k = 4 * ch + f
                    a(h[:, 0, k, :], bank[4 + f][:, :], ACT.Copy, scale=pcol[:, g2 + k:g2 + k + 1]).then_inc(h2_hi, 1)

            hi_chunks(S_WO + 1)
            act.wait_ge(half_ready[1], transposed_before(S_WO))
            act.dma_start(res[:, :, :], x.rearrange("(b p) n -> p b n", p=P)).then_inc(res_in, 16)
            act.dma_start(gfin[:, :], bass.AP(final_norm_g.tensor, 0, [[0, P], [1, D]])).then_inc(res_in, 16)
            hi_chunks(S_WO + 2)
            hi_chunks(S_WO + 3)
            norm_hi(0)
            hi_chunks(S_MLP)
            norm_hi(1)

            def mlp_quarter(it, first=False, last=False):
                for u in range(4):
                    hi_chunks(S_MLP + u + 1, 8, it)
                    for j in range(2):
                        act.wait_ge(half_ready[j], at(lambda v: v + 1, 33 + u, 4, it))
                        a(ta[:, j, :], bank[j][:, :], ACT.Relu).then_inc(free_act[j], 1)
                        act.wait_ge(sqr, index(it) * 8 + (2 * u + j + 1))
                        a(hid[:, 0, 2 * u + j, :], ty[:, j, :], ACT.Copy).then_inc(hid_hi, 1)
                    if first and u == 0:
                        for b in range(TB):
                            act.wait_ge(ss2_ready, b) if b else None
                            a(scratch, res[:, b, :], ACT.Square, accum_out=ss2[:, b:b + 1]).then_inc(ss2_ready, 1)
                for u in range(4):
                    if not (last and u == 3):
                        hi_chunks(S_MLP + u + 5, 8, it)
                    if last and u == 1:
                        for b in range(TB):
                            act.wait_ge(row_free, 8 * 4 + b + 1)
                            if b:
                                act.wait_ge(ss3_ready, b)
                            a(scratch[:, 0:512], res[:, b, 0:512], ACT.Square,
                              accum_out=ss3[:, 0, b:b + 1]).then_inc(ss3_ready, 1)
                        act.wait_ge(ss3_ready, TB)
                        a(rms3[:, 0, :], ss3[:, 0, :], ACT.Identity, bias=eps[:, :],
                          scale=1.0 / D).then_inc(root3_part, 1)
                    if last and u == 3:
                        act.wait_ge(root3_part, 1)
                        for b in range(TB):
                            act.wait_ge(row_free, 8 * 4 + 4 + b + 1)
                            act.wait_ge(ss3_ready, TB + b)
                            a(scratch[:, 0:512], res[:, b, 512:D], ACT.Square,
                              accum_out=ss3[:, 1, b:b + 1]).then_inc(ss3_ready, 1)
                            act.wait_ge(ss3_ready, TB + b + 1)
                            a(rms3[:, 1, b:b + 1], ss3[:, 1, b:b + 1], ACT.Sqrt, bias=rms3[:, 0, b:b + 1],
                              scale=1.0 / D).then_inc(root3_done, 1)
                            act.wait_ge(gained, b + 1)
                            act.wait_ge(fin_step, b + 1)
                            a(res[:, b, 0:512], res[:, b, 0:512], ACT.Copy,
                              scale=rms3[:, 2, b:b + 1]).then_inc(out_left, 1)

            mlp_quarter(0, first=True)
            with act.Fori(1, 3) as i:
                mlp_quarter(Pass(i, 1, 3))
            mlp_quarter(3, last=True)

        @block.vector
        def _(dve):
            v = nc.vector
            def lo_chunks(s, step=0, it=0, chunks=(0, 1)):
                s1 = s + step * first_of(it)
                for e in chunks:
                    wait(dve, hi_ready, at(lambda w: 2 * w + e + 1, s, step, it))
                    w = wgt[weight_slot(s1)]
                    v.tensor_tensor(w[:, 1, 1024 * e:1024 * e + 1024], raw[raw_slot(2 * s1 + e)][:, :],
                                    f32(w[:, 0, 1024 * e:1024 * e + 1024]), ALU.subtract).then_inc(lo_ready, 1)

            for b in range(TB):
                dve.wait_ge(root_done, b + 1)
                v.reciprocal(rms[:, 1, b:b + 1], rms[:, 0, b:b + 1]).then_inc(rms_step, 1)
                dve.wait_ge(rms_step, b + 1)
                v.tensor_scalar(xn[:, b, :], xn[:, b, :], rms[:, 1, b:b + 1], None, ALU.mult).then_inc(xn_ready, 1)
                if b == 1:
                    dve.wait_ge(par_t, 1)
                    v.tensor_copy(pcol[:, :], bank[KT - 1][:, 0:5 * KT]).then_inc(par_ready, 1)
            lo_chunks(S_KV, chunks=(0,))
            for k in range(KT):
                if k == KT // 2:
                    lo_chunks(S_KV, chunks=(1,))
                dve.wait_ge(h_hi, k + 1)
                v.scalar_tensor_tensor(out=h[:, 1, k, :], in0=bank[k][:, :], scalar=pcol[:, g1 + k:g1 + k + 1],
                                       in1=f32(h[:, 0, k, :]), op0=ALU.mult, op1=ALU.subtract).then_inc(h_ready, 1)
            lo_chunks(S_Q)
            for kg in range(KV):
                src = slice(HD * kg, HD * kg + HD)
                dve.wait_ge(k_hi, 2 * kg + 2)
                for up in range(2):
                    i = v.scalar_tensor_tensor(out=klo[HD * up:HD * up + HD, kg, :], in0=bank[1][src, :],
                                               scalar=SCALE, in1=f32(khi[src, kg, :]), op0=ALU.mult,
                                               op1=ALU.subtract)
            i.then_inc(free_dve[1], 1)
            with dve.Fori(0, 2) as i:
                for e in range(2):
                    lo_chunks(S_Q + 1 + e, 2, Pass(i, 0, 2))
                    dve.wait_ge(half_ready[1], i * 2 + (2 + e))
                    v.tensor_copy(qa[:, cols(i * 4 + (2 * e + 1), 1), :],
                                  bank[1][:, :].rearrange("p (a n) -> p a n", a=1)).then_inc(free_dve[1], 1)
            dve.wait_ge(vt_done, 1)
            v.tensor_copy(vnat[:, :, :], bank[B_VT][:, :].rearrange("p (b n) -> p b n", b=TB)).then_inc(v_ready, 1)

            def stage_queries(n):
                for par in range(2):
                    half, other = slice(HD * par, HD * par + HD), slice(HD - HD * par, 2 * HD - HD * par)
                    wait(dve, qs_hi, 2 * n + (par + 1))
                    v.tensor_tensor(qs[other, :, par, ::-1], qa[half, :, cols(n * P, P)], f32(qs[half, :, par, ::-1]),
                                    ALU.subtract).then_inc(qs_ready, 1)

            def stage_values(n):
                wait(dve, vs_hi, n + 1)
                for kb in keys_of(n)[0]:
                    i = v.tensor_tensor(vs[:, kb, :, 1, :],
                                        vnat[:, cols(n + kb - 1, 1), :].rearrange("p b (g d) -> p (b g) d", g=KV),
                                        f32(vs[:, kb, :, 0, :]), ALU.subtract)
                i.then_inc(vs_ready, 1)

            def add_bias(n, qd):
                wait_apart(dve, qk_ready, 4 * n + (qd + 1))
                _, lo = keys_of(n)
                for i in range(4):
                    head = 4 * qd + i
                    i_ = v.tensor_tensor_reduce(
                        out=pr[:, qd % 2, i, lo:2 * P],
                        in0=bank[B_SC + i // 2][:, 256 * (i % 2) + lo:256 * (i % 2) + 256],
                        in1=bias[:, head, lo:2 * P], scale=1.0, scalar=sink[:, head:head + 1], op0=ALU.add,
                        op1=ALU.max, accum_out=top_m[:, qd % 2, i:i + 1])
                i_.then_inc(logits, 1)
                wait(dve, logits, 4 * n + (qd + 1))
                v.tensor_scalar(neg_m[:, qd % 2, :], top_m[:, qd % 2, :], -1.0, None, ALU.mult)
                v.tensor_tensor(snk_d[:, qd % 2, :], sink[:, 4 * qd:4 * qd + 4], top_m[:, qd % 2, :],
                                ALU.subtract).then_inc(shift_ready, 1)

            def normalise(n, qd):
                s = qd % 2
                wait(dve, exp_ready, 4 * n + (qd + 1))
                v.tensor_tensor(tot[:, s, :], den[:, s, :], snk_d[:, s, :], ALU.add).then_inc(tot_ready, 1)
                wait(dve, tot_ready, 4 * n + (qd + 1))
                v.reciprocal(rec[:, s, :], tot[:, s, :]).then_inc(rec_ready, 1)
                wait(dve, rec_ready, 4 * n + (qd + 1))
                _, lo = keys_of(n)
                for i in range(4):
                    w = pr[:, s, i, lo:2 * P]
                    i_ = v.tensor_scalar(w, w, rec[:, s, i:i + 1], None, ALU.mult)
                i_.then_inc(p_ready, 1)

            def probs_lo(n, qd):
                kbs, _ = keys_of(n)
                for kb in kbs:
                    wait(dve, pt_hi, 8 * n + (2 * qd + kb + 1))
                    v.tensor_tensor(pt[:, 1, kb, :], bank[B_PT + kb][:, :], f32(pt[:, 0, kb, :]),
                                    ALU.subtract).then_inc(pt_ready, 2 // len(kbs))

            def attention_out(n, qd):
                wait_apart(dve, low_out, 4 * n + (qd + 1))
                for par in range(2):
                    hi, lo = (t[0:HD, 256 * par:256 * par + 256].rearrange("p (a n) -> p a n", a=2)[:, :, ::-1]
                              for t in (bank[B_PV], pv_low))
                    i = v.tensor_tensor(qa[HD * par:HD * par + HD, 2 * qd:2 * qd + 2, cols(n * P, P)], hi, lo, ALU.add)
                i.then_inc(pv_out, 1)

            def conv(n, it, j):
                dve.wait_ge(half_ready[j], at(lambda w: w + 1, 6, 3, it))
                dve.wait_ge(free_act[j], at(lambda w: frees("A", j, w), 5, 3, it))
                v.tensor_tensor(tz[:, j, 2:T + 2], bank[j][:, :], ta[:, j, :], ALU.mult).then_inc(free_dve[j], 1)
                dve.wait_ge(free_dve[j], at(lambda w: frees("D", j, w), 6, 3, it))

                def tap(i):
                    return pcol[:, cols(n * 2 + (j + (2 + i) * KT), 1)]
                v.tensor_scalar(ty[:, j, :], tz[:, j, 2:T + 2], tap(2), None, ALU.mult).then_inc(conv1, 1)
                for i in (1, 0):
                    dve.wait_ge(conv1, n * 6 + (3 * j + 2 - i))
                    v.scalar_tensor_tensor(out=ty[:, j, :], in0=tz[:, j, i:T + i], scalar=tap(i), in1=ty[:, j, :],
                                           op0=ALU.mult, op1=ALU.add).then_inc(conv1, 1)

            def conv_gate(n, it, j):
                dve.wait_ge(half_ready[j], at(lambda w: w + 1, 7, 3, it))
                wait(dve, conv1, n * 6 + (3 * j + 3))
                v.tensor_tensor(y[:, cols(n * 2 + j, 1), :], bank[j][:, :].rearrange("p (a n) -> p a n", a=1),
                                ty[:, j:j + 1, :], ALU.mult).then_inc(free_dve[j], 1)

            def mixer_block(n, it, before):
                first = before is None
                if not first:
                    probs_lo(before, 2)
                stage_queries(n)
                lo_chunks(S_MIX + 1, 3, it)
                if not first:
                    attention_out(before, 2)
                add_bias(n, 0)
                if not first:
                    probs_lo(before, 3)
                lo_chunks(S_MIX + 2, 3, it)
                if not first:
                    attention_out(before, 3)
                add_bias(n, 1)
                normalise(n, 0)
                stage_values(n)
                conv(n, it, 0)
                probs_lo(n, 0)
                conv(n, it, 1)
                add_bias(n, 2)
                normalise(n, 1)
                lo_chunks(S_MIX + 3, 3, it)
                attention_out(n, 0)
                conv_gate(n, it, 0)
                probs_lo(n, 1)
                normalise(n, 2)
                add_bias(n, 3)
                conv_gate(n, it, 1)
                attention_out(n, 1)
                normalise(n, 3)

            dve.wait_ge(bias_in, 16)
            dve.wait_ge(zeroed, N_ZEROED)
            mixer_block(0, 0, None)
            with dve.Fori(1, TB) as n:
                mixer_block(n, Pass(n, 1, TB), n - 1)

            def split(dst, src, e, done):
                dve.wait_ge(sp_hi, done + 1)
                v.tensor_tensor(dst[:, 1, 4 * e:4 * e + 4, :], src[:, 4 * e:4 * e + 4, :],
                                f32(dst[:, 0, 4 * e:4 * e + 4, :]), ALU.subtract).then_inc(sp_ready, 1)

            def branch_group(it, first):
                i = index(it)
                if first:
                    probs_lo(3, 2)
                lo_chunks(S_OUT + 1, 4, it)
                if first:
                    split(ysplit, y, 0, 0)
                    attention_out(3, 2)
                    probs_lo(3, 3)
                    split(ysplit, y, 1, 1)
                    attention_out(3, 3)
                lo_chunks(S_OUT + 2, 4, it)
                if first:
                    split(asplit, qa, 0, 2)
                    split(asplit, qa, 1, 3)
                for j in range(2):
                    dve.wait_ge(half_ready[j], at(lambda w: w + 1, 18, 4, it))
                    dve.wait_ge(free_act[j], at(lambda w: frees("A", j, w), 17, 4, it))
                    v.tensor_tensor(tz[:, j, 0:T], bank[j][:, :], ta[:, j, :], ALU.mult).then_inc(free_dve[j], 1)
                lo_chunks(S_OUT + 3, 4, it)
                lo_chunks(S_OUT + 4, 4, it)
                for j in range(2):
                    dve.wait_ge(half_ready[j], at(lambda w: w + 1, 20, 4, it))
                    dve.wait_ge(free_act[j], at(lambda w: frees("A", j, w), 19, 4, it))
                    v.tensor_tensor(ty[:, j, :], bank[j][:, :], ta[:, j, :], ALU.mult).then_inc(free_dve[j], 1)
                    dve.wait_ge(free_dve[j], at(lambda w: frees("D", j, w), 20, 4, it))
                    v.tensor_tensor(ty[:, j, :], ty[:, j, :], tz[:, j, 0:T], ALU.add).then_inc(mix_f, 1)
                    dve.wait_ge(mix_f, i * 2 + (j + 1))
                    dve.wait_ge(mix_hi, i * 2 + (j + 1))
                    v.tensor_tensor(mix[:, 1, cols(i * 2 + j, 1), :], ty[:, j:j + 1, :],
                                    f32(mix[:, 0, cols(i * 2 + j, 1), :]), ALU.subtract).then_inc(mix_ready, 1)

            branch_group(0, True)
            with dve.Fori(1, 4) as j:
                branch_group(Pass(j, 1, 4), False)

            def norm_lo(ch):
                for f in range(4):
                    k = 4 * ch + f
                    dve.wait_ge(h2_hi, k + 1)
                    v.scalar_tensor_tensor(out=h[:, 1, k, :], in0=bank[4 + f][:, :], scalar=pcol[:, g2 + k:g2 + k + 1],
                                           in1=f32(h[:, 0, k, :]), op0=ALU.mult, op1=ALU.subtract).then_inc(h2_ready, 1)

            def add_mixers(ch):
                for b in range(TB):
                    dve.wait_ge(row_ready, 4 * ch + b + 1)
                    r = res[:, b, 512 * ch:512 * ch + 512]
                    v.tensor_tensor(r, bank[4 + b if ch == 0 else b][:, :], r, ALU.add).then_inc(row_free, 1)

            lo_chunks(S_WO + 1)
            dve.wait_ge(res_in, 32)
            lo_chunks(S_WO + 2)
            add_mixers(0)
            lo_chunks(S_WO + 3)
            norm_lo(0)
            lo_chunks(S_MLP)
            add_mixers(1)
            norm_lo(1)

            def add_mlp(i, ch, b):
                wait(dve, row_ready, i * 8 + (8 + 4 * ch + b + 1))
                r = res[:, b, 512 * ch:512 * ch + 512]
                v.scalar_tensor_tensor(out=r, in0=bank[4 + b if ch == 0 else b][:, :], scalar=rr2[:, 1, b:b + 1],
                                       in1=r, op0=ALU.mult, op1=ALU.add).then_inc(row_free, 1)

            def final_norm(b):
                dve.wait_ge(root3_done, b + 1)
                v.reciprocal(rms3[:, 2, b:b + 1], rms3[:, 1, b:b + 1]).then_inc(fin_step, 1)
                dve.wait_ge(fin_step, b + 1)
                r = res[:, b, 512:D]
                v.scalar_tensor_tensor(out=r, in0=r, scalar=rms3[:, 2, b:b + 1], in1=gfin[:, 512:D],
                                       op0=ALU.mult, op1=ALU.mult).then_inc(out_right, 1)

            def mlp_quarter(it, first=False, last=False):
                i = index(it)
                for u in range(4):
                    lo_chunks(S_MLP + u + 1, 8, it)
                    for j in range(2):
                        dve.wait_ge(free_act[j], at(lambda w: frees("A", j, w), 33 + u, 4, it))
                        v.tensor_tensor(ty[:, j, :], ta[:, j, :], ta[:, j, :], ALU.mult).then_inc(sqr, 1)
                        wait(dve, sqr, i * 8 + (2 * u + j + 1))
                        wait(dve, hid_hi, i * 8 + (2 * u + j + 1))
                        v.tensor_tensor(hid[:, 1, 2 * u + j, :], ty[:, j, :], f32(hid[:, 0, 2 * u + j, :]),
                                        ALU.subtract).then_inc(hid_ready, 1)
                    if first and u == 0:
                        dve.wait_ge(ss2_ready, TB)
                        v.tensor_scalar(rr2[:, 0, :], ss2[:, :], 1.0 / D, EPS, ALU.mult, ALU.add).then_inc(rr2_step, 1)
                        dve.wait_ge(rr2_step, 1)
                        v.reciprocal(rr2[:, 1, :], rr2[:, 0, :]).then_inc(rr2_step, 1)
                        dve.wait_ge(rr2_step, 2)
                for u in range(4):
                    if not (last and u == 3):
                        lo_chunks(S_MLP + u + 5, 8, it)
                    if last and u == 2:
                        for b in range(TB):
                            dve.wait_ge(ss3_ready, b + 1)
                            r = res[:, b, 0:512]
                            v.tensor_tensor(r, r, gfin[:, 0:512], ALU.mult).then_inc(gained, 1)
                    if u % 2 == 1:
                        for b in range(TB):
                            add_mlp(i, u // 2, b)
                            if last and u == 3:
                                final_norm(b)

            mlp_quarter(0, first=True)
            with dve.Fori(1, 3) as i:
                mlp_quarter(Pass(i, 1, 3))
            mlp_quarter(3, last=True)


INPUTS = ["x", "attn_norm_g", "w_in", "conv_w", "w_conv_out", "attn_sinks", "rel_bias", "w_attn_out", "w_o",
          "mlp_norm_g", "w_up", "w_down", "final_norm_g"]


def kernel(**inputs):
    import concourse.bacc as bacc
    from concourse.bass_utils import run_bass_kernel_spmd

    nc = bacc.Bacc("TRN2", target_bir_lowering=False, num_devices=1)
    arrays, args = {}, []
    for name in INPUTS:
        v = np.ascontiguousarray(inputs[name])
        arrays[f"in_{name}"] = v
        t = nc.dram_tensor(f"in_{name}", v.shape, mybir.dt.from_np(v.dtype), kind="ExternalInput").ap()
        drop = name in ("x", "w_in", "w_conv_out", "w_attn_out", "w_o", "w_up", "w_down")
        args.append(t.rearrange("a b c -> (a b) c") if drop else t)
    result = nc.dram_tensor("out_0", (1, T, D), F32, kind="ExternalOutput").ap()
    build(nc, *args, result.rearrange("a b c -> (a b) c"))
    r = run_bass_kernel_spmd(nc, [arrays], core_ids=[0])
    return r.results[0]["out_0"]
```
